# Optimizing a Trainium2 kernel written in Bass

```python
import math
import jax, jax.numpy as jnp
from jax import lax
import numpy as np

D_MODEL = 1024
BATCH = 1
SEQ = 2048
DEPTH = 1

CHUNK = 64
N_META = 16
N_MIXERS = 3
POOL_WINDOWS = (2, 4, 8, 16)
N_POOL_GROUPS = len(POOL_WINDOWS)
POOL_GROUP = D_MODEL // N_POOL_GROUPS
N_HEADS = 8
HEAD_DIM = D_MODEL // N_HEADS
KV_LATENT = D_MODEL // 4
IDX_HEADS = 8
IDX_DIM = 64
TOPK_MAX = 256
Q_BLOCK = 128
CONV_WIDTH = 3
D_FF = -(-8 * D_MODEL // (3 * 256)) * 256
B_PROJ = D_MODEL + KV_LATENT + IDX_HEADS * IDX_DIM + IDX_DIM + IDX_HEADS
ALPHA = (2.0 * DEPTH) ** 0.25
BETA = (8.0 * DEPTH) ** -0.25
LN_EPS = 1e-5

kernel_name = "hybrid_pool_dsa_shortconv_deepnorm_trunk"

def _n_of_kind(kind):
    return (DEPTH - kind + N_MIXERS - 1) // N_MIXERS

def _chunk_ids(t):
    pos = jnp.arange(t)
    return jnp.where(pos < N_META, 0, 1 + (pos - N_META) // CHUNK)

def layer_norm(x, g, b):
    xf = x.astype(jnp.float32)
    mu = jnp.mean(xf, axis=-1, keepdims=True)
    var = jnp.mean(jnp.square(xf - mu), axis=-1, keepdims=True)
    y = (xf - mu) * lax.rsqrt(var + LN_EPS) * g.astype(jnp.float32) + b.astype(jnp.float32)
    return y.astype(x.dtype)

def swiglu_ffn(x, w_gu, w_down):
    gate, up = jnp.split(x @ w_gu, 2, axis=-1)
    return (jax.nn.silu(gate) * up) @ w_down

def pool_mixer(x, w_in, w_group, scale, w_out):
    b, t, _ = x.shape
    u = (x @ w_in).reshape(b, t, N_POOL_GROUPS, POOL_GROUP)
    cs = jnp.cumsum(u.astype(jnp.float32), axis=1)
    cs = jnp.pad(cs, ((0, 0), (1, 0), (0, 0), (0, 0)))
    hi = jnp.arange(t) + 1
    pooled = []
    for g, w in enumerate(POOL_WINDOWS):
        lo = jnp.maximum(hi - w, 0)
        win = cs[:, hi, g] - cs[:, lo, g]
        pooled.append(win / (hi - lo).astype(jnp.float32)[None, :, None])
    pooled = jnp.stack(pooled, axis=2).astype(x.dtype)
    y = jnp.einsum('btgc,gce->btge', pooled - u, w_group).reshape(b, t, D_MODEL)
    return (y * scale) @ w_out

def short_conv_mixer(x, w_in, conv_w, w_out):
    t = x.shape[1]
    bg, cg, hv = jnp.split(x @ w_in, 3, axis=-1)
    z = jnp.pad(cg * hv, ((0, 0), (CONV_WIDTH - 1, 0), (0, 0)))
    conv = sum(z[:, k:k + t] * conv_w[k] for k in range(CONV_WIDTH))
    return (bg * conv) @ w_out

def dsa_mixer(x, n_keys, w_in, w_uk, w_uv, w_out):
    b, t, _ = x.shape
    topk = min(TOPK_MAX, n_keys // 4)
    proj = x @ w_in
    o = 0
    q = proj[..., o:o + D_MODEL].reshape(b, t, N_HEADS, HEAD_DIM); o += D_MODEL
    c_kv = proj[..., o:o + KV_LATENT]; o += KV_LATENT
    q_idx = proj[..., o:o + IDX_HEADS * IDX_DIM].reshape(b, t, IDX_HEADS, IDX_DIM); o += IDX_HEADS * IDX_DIM
    k_idx = proj[..., o:o + IDX_DIM].astype(jnp.float32); o += IDX_DIM
    w_idx = proj[..., o:o + IDX_HEADS]

    nblk = -(-t // Q_BLOCK)
    tp = nblk * Q_BLOCK
    cid_all = _chunk_ids(tp)
    cid_k = cid_all[:t]

    def to_blocks(a):
        a = jnp.pad(a, [(0, 0), (0, tp - t)] + [(0, 0)] * (a.ndim - 2))
        return jnp.moveaxis(a.reshape(b, nblk, Q_BLOCK, *a.shape[2:]), 1, 0)

    def attend_block(args):
        qb, qib, wib, cq = args
        s = jnp.einsum('bqhd,bsd->bqhs', qib.astype(jnp.float32), k_idx)
        score = jnp.einsum('bqhs,bqh->bqs', jax.nn.relu(s), wib.astype(jnp.float32))
        allowed = cid_k[None, :] <= cq[:, None]
        score = jnp.where(allowed[None], score, -jnp.inf)
        top_val, top_idx = lax.top_k(score, topk)
        valid = top_val > -jnp.inf
        kv_sel = jax.vmap(lambda c, i: c[i])(c_kv, top_idx)
        q_lat = jnp.einsum('bqhd,hdl->bqhl', qb, w_uk)
        logits = jnp.einsum('bqhl,bqkl->bqhk', q_lat, kv_sel).astype(jnp.float32)
        logits = jnp.where(valid[:, :, None, :], logits * (HEAD_DIM ** -0.5), -jnp.inf)
        p = jax.nn.softmax(logits, axis=-1).astype(kv_sel.dtype)
        return jnp.einsum('bqhk,bqkl->bqhl', p, kv_sel)

    ctx = lax.map(attend_block, (to_blocks(q), to_blocks(q_idx), to_blocks(w_idx),
                                 cid_all.reshape(nblk, Q_BLOCK)))
    ctx = jnp.moveaxis(ctx, 0, 1).reshape(b, tp, N_HEADS, KV_LATENT)[:, :t]
    out = jnp.einsum('bthl,hld->bthd', ctx, w_uv).reshape(b, t, D_MODEL)
    return out @ w_out

def setup_inputs(seed: int = 0) -> dict:
    key = jax.random.key(seed)
    ks = iter(jax.random.split(key, 32))
    n_a, n_b, n_c = _n_of_kind(0), _n_of_kind(1), _n_of_kind(2)

    def nrm(shape, scale):
        return jax.random.normal(next(ks), shape, jnp.float32) * scale

    def near_one(shape):
        return 1.0 + nrm(shape, 0.02)

    d = D_MODEL
    return {
        "x": nrm((BATCH, SEQ, d), 1.0),
        "meta": nrm((N_META, d), 1.0),
        "a_w_in": nrm((n_a, d, d), d ** -0.5),
        "a_w_group": nrm((n_a, N_POOL_GROUPS, POOL_GROUP, POOL_GROUP), POOL_GROUP ** -0.5),
        "a_scale": near_one((n_a, d)),
        "a_w_out": nrm((n_a, d, d), BETA * d ** -0.5),
        "b_w_in": nrm((n_b, d, B_PROJ), d ** -0.5),
        "b_w_uk": nrm((n_b, N_HEADS, HEAD_DIM, KV_LATENT), HEAD_DIM ** -0.5),
        "b_w_uv": nrm((n_b, N_HEADS, KV_LATENT, HEAD_DIM), KV_LATENT ** -0.5),
        "b_w_out": nrm((n_b, d, d), BETA * d ** -0.5),
        "c_w_in": nrm((n_c, d, 3 * d), d ** -0.5),
        "c_conv": nrm((n_c, CONV_WIDTH, d), CONV_WIDTH ** -0.5),
        "c_w_out": nrm((n_c, d, d), BETA * d ** -0.5),
        "ln_mix_g": near_one((DEPTH, d)),
        "ln_mix_b": nrm((DEPTH, d), 0.02),
        "ffn_w_gu": nrm((DEPTH, d, 2 * D_FF), d ** -0.5),
        "ffn_w_down": nrm((DEPTH, D_FF, d), BETA * D_FF ** -0.5),
        "ln_ffn_g": near_one((DEPTH, d)),
        "ln_ffn_b": nrm((DEPTH, d), 0.02),
    }

def reference(x, meta, a_w_in, a_w_group, a_scale, a_w_out, b_w_in, b_w_uk, b_w_uv,
              b_w_out, c_w_in, c_conv, c_w_out, ln_mix_g, ln_mix_b, ffn_w_gu,
              ffn_w_down, ln_ffn_g, ln_ffn_b):
    b, seq, d = x.shape
    h = jnp.concatenate([jnp.broadcast_to(meta[None].astype(x.dtype), (b, N_META, d)), x], axis=1)
    for i in range(DEPTH):
        kind, j = i % N_MIXERS, i // N_MIXERS
        if kind == 0:
            m = pool_mixer(h, a_w_in[j], a_w_group[j], a_scale[j], a_w_out[j])
        elif kind == 1:
            m = dsa_mixer(h, seq, b_w_in[j], b_w_uk[j], b_w_uv[j], b_w_out[j])
        else:
            m = short_conv_mixer(h, c_w_in[j], c_conv[j], c_w_out[j])
        h = layer_norm(ALPHA * h + m, ln_mix_g[i], ln_mix_b[i])
        h = layer_norm(ALPHA * h + swiglu_ffn(h, ffn_w_gu[i], ffn_w_down[i]), ln_ffn_g[i], ln_ffn_b[i])
    return h[:, N_META:]


_drawn_inputs = setup_inputs


def setup_inputs(seed=0):
    import zlib

    import numpy as np

    out = dict(_drawn_inputs(seed))
    spreads = {}
    factors = {'meta': 8.0, 'a_scale': 6.832, 'ln_mix_b': 2.743, 'ln_ffn_g': 2.882, 'ln_ffn_b': 2.903}
    for name, (base, spread) in spreads.items():
        noise = np.random.default_rng([zlib.crc32(name.encode()), seed]).standard_normal(out[name].shape)
        drawn = base * np.exp(spread * noise) if base else spread * noise
        out[name] = __import__('jax').numpy.asarray(drawn.astype(out[name].dtype))
    for name, factor in factors.items():
        out[name] = (out[name] * factor).astype(out[name].dtype)
    return out
```

```python
import math
from contextlib import ExitStack

import concourse.bass as bass
from concourse import mybir

F32 = mybir.dt.float32
F32R = mybir.dt.float32r
ALU = mybir.AluOpType
ACT = mybir.ActivationFunctionType

P = 128
TOK = 512
CW = 256
WINDOWS = (2, 4, 8, 16)
GROUPS = len(WINDOWS)
EPS = 1e-5
ALPHA = 2.0 ** 0.25
H = max(WINDOWS)


def trunk(nc, x, meta, w_in, w_group, scale, w_out, mix_g, mix_b, w_gu, w_down, ffn_g, ffn_b, out,
          fold_dram, h_dram):
    SEQ, D = x.shape
    N_META = meta.shape[0]
    FF = w_down.shape[0]
    KT = D // P
    FT = FF // P
    BLOCKS = SEQ // TOK
    TT = TOK // P
    PAIRS = D // CW
    JF = FF // CW
    DN = -(-FT // KT)
    KS = [min(KT, FT - KT * t) for t in range(DN)]
    assert KT == 8 and PAIRS == GROUPS == TT and N_META == H and D // GROUPS == CW

    MIX0 = GROUPS
    FFN0 = MIX0 + 2 * PAIRS * BLOCKS
    PER_FFN = 2 * JF + PAIRS * DN
    assert MIX0 % 2 == 0 and FFN0 % 2 == 0 and PER_FFN % 2 == 0

    def c_in(b, i):
        return b * (2 * PAIRS) + (MIX0 + i)

    def c_mix(b, i):
        return b * (2 * PAIRS) + (MIX0 + PAIRS + i)

    def c_gu(b, j, up):
        return b * PER_FFN + j * 2 + (FFN0 + up)

    def c_dn(b, p, t):
        return b * PER_FFN + (FFN0 + 2 * JF + DN * p + t)

    TURN0 = GROUPS + 2

    def turn_x(b):
        return b * (2 * TT) + TURN0

    x_rows = x.rearrange("(n p) d -> p n d", p=P)
    h_rows = h_dram.rearrange("(n p) d -> p n d", p=P)
    out_rows = out.rearrange("(n p) d -> p n d", p=P)
    win_v = w_in.rearrange("(k p) n -> p k n", p=P)
    wgu_v = w_gu.rearrange("(k p) n -> p k n", p=P)
    wdn_v = w_down.rearrange("(k p) n -> p k n", p=P)
    wout_v = w_out.rearrange("(k p) n -> p k n", p=P)
    fold_v = fold_dram.rearrange("(k p) n -> p k n", p=P)
    group_v = w_group.rearrange("g (t p) e -> p (g t) e", p=P)

    with ExitStack() as ctx:
        def sb(name, shape, dt=F32):
            return ctx.enter_context(nc.sbuf_tensor(name, shape, dt))

        def sem(name):
            return ctx.enter_context(nc.semaphore(name))

        act_base = -(-nc.sbuf_base // 32) * 32
        act_sb = sb("act_sb", [P, FT, 2, TOK], F32R)
        assert nc.sbuf_base == act_base + FT * 2 * TOK * 4
        spare = act_base + (KT + 2 * GROUPS) * 2 * TOK * 4
        sums = [nc.alloc_sbuf_tensor_at(f"sums{n}", [P, 2, H + TOK], F32, offset=spare + n * 2 * (H + TOK) * 4)
                for n in range(2)]
        fold_st = nc.alloc_sbuf_tensor_at("fold_st", [P, 2, 2, D], F32, offset=spare)
        assert spare + 4 * D * 4 <= act_base + FT * 2 * TOK * 4
        mov = sb("mov", [P, KT, 2, TOK], F32R)
        split = sb("split", [P, 2, 2, KT * CW], F32R)
        raw = sb("raw", [P, 2, KT * CW])
        z = sb("z", [P, TT, D])
        nat = sb("nat", [P, 2, D])
        gb = sb("gb", [P, 2, D])
        stage = sb("stage", [P, 2, H + TOK])
        hist = sb("hist", [P, KT, H])
        meta_t = sb("meta_t", [P, KT, 2, N_META], F32R)
        ident = sb("ident", [P, P])
        scale_sb = sb("scale_sb", [P, KT])
        stats = sb("stats", [P, TT, PAIRS, 6])
        mv = sb("mv", [P, TT, 2])
        var_eps = sb("var_eps", [P, TT])
        rstd = sb("rstd", [P, TT])
        minus_half = sb("minus_half", [P, TT])

        acc = ctx.enter_context(nc.psum_tensor("acc", [P, 4, TOK], F32))
        turn = ctx.enter_context(nc.psum_tensor("turn", [P, 2, TOK], F32))
        back = ctx.enter_context(nc.psum_tensor("back", [P, 2, TOK], F32))

        raw_landed = [sem("raw_landed0"), sem("raw_landed1")]
        nat_landed = [sem("nat_landed0"), sem("nat_landed1")]
        z_landed = sem("z_landed")
        group_landed = sem("group_landed")
        meta_landed = sem("meta_landed")
        scale_landed = sem("scale_landed")
        gb_landed = sem("gb_landed")
        fold_stored = [sem("fold_stored0"), sem("fold_stored1")]
        rows_stored = sem("rows_stored")
        ident_zero = sem("ident_zero")
        ident_ready = sem("ident_ready")
        half_ready = sem("half_ready")
        raw_scaled = sem("raw_scaled")
        w_hi_ready = sem("w_hi_ready")
        w_lo_ready = sem("w_lo_ready")
        chunk_done = sem("chunk_done")
        fold_a_staged = sem("fold_a_staged")
        fold_b_staged = sem("fold_b_staged")
        turn_done = sem("turn_done")
        turn_hi_ready = sem("turn_hi_ready")
        turn_lo_ready = sem("turn_lo_ready")
        meta_u_done = sem("meta_u_done")
        meta_u_taken = sem("meta_u_taken")
        u_staged = sem("u_staged")
        pool_link = sem("pool_link")
        d_ready = sem("d_ready")
        d_hi_ready = sem("d_hi_ready")
        d_lo_ready = sem("d_lo_ready")
        y_staged = sem("y_staged")
        back_done = sem("back_done")
        added = sem("added")
        silu_done = sem("silu_done")
        a_ready = sem("a_ready")
        a_hi_ready = sem("a_hi_ready")
        a_lo_ready = sem("a_lo_ready")
        stats_done = sem("stats_done")
        aggr_done = sem("aggr_done")
        var_ready = sem("var_ready")
        rstd_ready = sem("rstd_ready")
        centered = sem("centered")
        ln_applied = sem("ln_applied")

        block = ctx.enter_context(nc.Block())

        def pair(c2):
            return acc[:, 2 * c2:2 * c2 + 2, :]

        def staged():
            return stage[:, :, H:H + TOK]

        def f32(ap):
            return ap.bitcast(F32)

        @block.sync
        def _(sp):
            def load_chunk(c, slot, src, width=CW):
                if not (isinstance(c, int) and c < 2):
                    sp.wait_ge(w_lo_ready, c - 1)
                k = src.shape[1]
                dst = raw[:, slot, 0:k * width].rearrange("p (k n) -> p k n", n=width)
                sp.dma_start(dst, src).then_inc(raw_landed[slot], 16)

            def load_nat(rows, m, slot, tile):
                if not (isinstance(m, int) and m < 2):
                    sp.wait_ge(turn_done, m * 2 + (TURN0 - 2))
                sp.dma_start(nat[:, slot, :], rows[:, bass.ds(tile, 1), :].rearrange("p a d -> p (a d)")
                             ).then_inc(nat_landed[slot], 16)

            def load_z(rows, stage_no, b):
                if not (isinstance(stage_no, int) and stage_no == 0):
                    sp.wait_ge(rows_stored, stage_no * (16 * TT))
                sp.dma_start(z[:], rows[:, bass.ds(b * TT, TT), :]).then_inc(z_landed, 16)

            def store_rows(rows, stage_no, b, j):
                sp.wait_ge(ln_applied, stage_no * TT + (j + 1))
                sp.dma_start(rows[:, bass.ds(b * TT + j, 1), :].rearrange("p a d -> p (a d)"),
                             z[:, j, :]).then_inc(rows_stored, 16)

            def fold_chunk(g):
                load_chunk(g, g % 2, wout_v[:, 2 * g:2 * g + 2, :], D)

            def in_chunk(b, i):
                g = GROUPS - 1 - i
                load_chunk(c_in(b, i), i % 2, win_v[:, :, g * CW:(g + 1) * CW])

            def mix_chunk(b, i):
                load_chunk(c_mix(b, i), i % 2, fold_v[:, :, i * CW:(i + 1) * CW])

            def store_fold(g):
                sp.wait_ge(fold_a_staged, g + 1)
                sp.wait_ge(fold_b_staged, g + 1)
                row = 2 * (GROUPS - 1 - g)
                for t in range(2):
                    sp.dma_start(fold_v[:, row + t, :], fold_st[:, g % 2, t, :]).then_inc(fold_stored[g % 2], 16)

            sp.dma_start(z[:, 0:2, :].rearrange("p a (b e) -> p (a b) e", e=CW), group_v).then_inc(group_landed, 16)
            sp.dma_start(scale_sb[:], scale).then_inc(scale_landed, 16)
            fold_chunk(0)
            sp.dma_start(z[0:N_META, 2, :], meta).then_inc(meta_landed, 16)
            fold_chunk(1)
            load_nat(x_rows, 0, 0, 0)
            fold_chunk(2)
            load_nat(x_rows, 1, 1, 1)
            fold_chunk(3)
            load_nat(x_rows, 2, 0, 2)
            in_chunk(0, 0)
            store_fold(0)
            load_nat(x_rows, 3, 1, 3)
            in_chunk(0, 1)
            store_fold(1)
            for n, v in enumerate((mix_g, mix_b)):
                sp.dma_start(gb[:, n, :], v.partition_broadcast(P)).then_inc(gb_landed, 16)
            in_chunk(0, 2)
            store_fold(2)
            in_chunk(0, 3)
            store_fold(3)
            sp.wait_ge(turn_done, TURN0)
            load_z(x_rows, 0, 0)
            for n in range(2):
                sp.wait_ge(fold_stored[n], 16 * GROUPS)

            def next_nat(b, i, last):
                if last:
                    if i == 0:
                        sp.wait_ge(rows_stored, 16 * TT)
                    load_nat(h_rows, BLOCKS * TT + i, i % 2, i)
                else:
                    load_nat(x_rows, (b + 1) * TT + i, i % 2, (b + 1) * TT + i)

            def mixer_block(b, first=False, last=False):
                if not first:
                    for i in range(PAIRS):
                        in_chunk(b, i)
                    for j in range(1):
                        store_rows(h_rows, b - 1, b - 1, j)
                mix_chunk(b, 0)
                next_nat(b, 0, last)
                mix_chunk(b, 1)
                next_nat(b, 1, last)
                if not first:
                    store_rows(h_rows, b - 1, b - 1, 1)
                mix_chunk(b, 2)
                if not first:
                    store_rows(h_rows, b - 1, b - 1, 2)
                    store_rows(h_rows, b - 1, b - 1, 3)
                    load_z(x_rows, b, b)
                next_nat(b, 2, last)
                mix_chunk(b, 3)
                next_nat(b, 3, last)

            mixer_block(0, first=True)
            with sp.Fori(1, BLOCKS - 1) as b:
                mixer_block(b)
            mixer_block(BLOCKS - 1, last=True)

            def gu_chunks(b, j):
                for up in range(2):
                    load_chunk(c_gu(b, j, up), up, wgu_v[:, :, bass.ds(j * CW + up * FF, CW)])

            def ffn_block(b, first=False, last=False):
                rows, row_b = (h_rows, BLOCKS - 1) if first else (out_rows, b - 1)
                gu_chunks(b, 0)
                for j in range(1, 1 + TT):
                    gu_chunks(b, j)
                    store_rows(rows, b + (BLOCKS - 1), row_b, j - 1)
                if first:
                    for n, v in enumerate((ffn_g, ffn_b)):
                        sp.dma_start(gb[:, n, :], v.partition_broadcast(P)).then_inc(gb_landed, 16)
                load_z(h_rows, b + BLOCKS, b)
                with sp.Fori(1 + TT, JF) as j:
                    gu_chunks(b, j)
                for p in range(PAIRS):
                    for t in range(DN):
                        load_chunk(c_dn(b, p, t), (DN * p + t) % 2,
                                   wdn_v[:, KT * t:KT * t + KS[t], p * CW:(p + 1) * CW])
                        if t == 1 and not last:
                            load_nat(h_rows, (b + 1 + BLOCKS) * TT + p, p % 2, (b + 1) * TT + p)

            ffn_block(0, first=True)
            with sp.Fori(1, BLOCKS - 1) as b:
                ffn_block(b)
            ffn_block(BLOCKS - 1, last=True)
            for j in range(TT):
                store_rows(out_rows, 2 * BLOCKS - 1, BLOCKS - 1, j)
            sp.wait_ge(rows_stored, 2 * BLOCKS * TT * 16)

        @block.gpsimd
        def _(pool):
            nc.gpsimd.memset(ident[:], 0.0).then_inc(ident_zero, 1)
            pool.wait_ge(ident_zero, 1)
            nc.gpsimd.affine_select(out=ident[:], in_=ident[:], compare_op=ALU.not_equal, fill=1.0, base=0,
                                    pattern=[[-1, P]], channel_multiplier=1).then_inc(ident_ready, 1)
            nc.gpsimd.memset(minus_half[:], -0.5).then_inc(half_ready, 1)
            pool.wait_ge(half_ready, 1)
            with pool.Fori(0, 2 * BLOCKS) as s:
                pool.wait_ge(var_ready, s + 1)
                nc.gpsimd.tensor_tensor(rstd[:], var_eps[:], minus_half[:], ALU.pow).then_inc(rstd_ready, 1)

        @block.tensor
        def _(pe):
            def turn_unit(unit, bank, blocks, width):
                if not (isinstance(unit, int) and unit < 2):
                    pe.wait_ge(turn_lo_ready, unit - 1)
                for n, blk in enumerate(blocks):
                    rows = blk.shape[0]
                    mm = nc.tensor.transpose(turn[:, bank, n * width:(n + 1) * width], blk, ident[0:rows, 0:rows])
                mm.then_inc(turn_done, 1)

            def turn_tile(b, i):
                pe.wait_ge(nat_landed[i % 2], b * (16 * TT // 2) + 16 * (i // 2 + 1))
                for h in range(2):
                    turn_unit(turn_x(b) + (2 * i + h), h,
                              [nat[:, i % 2, k * P:(k + 1) * P] for k in range(4 * h, 4 * h + 4)], P)

            def turn_back(s, p):
                pe.wait_ge(y_staged, s * PAIRS + (p + 1))
                for m in range(2):
                    if not (isinstance(s, int) and s == 0 and p == 0):
                        pe.wait_ge(added, s * (2 * PAIRS) + (2 * p + m - 1))
                    for j in range(TT):
                        mm = nc.tensor.transpose(back[:, m, j * P:(j + 1) * P],
                                                 stage[:, m, H + j * P:H + (j + 1) * P], ident[:])
                    mm.then_inc(back_done, 1)

            def products(c, slot, banks, moving, kn, first=True, final=True, before=None, between=None):
                pe.wait_ge(w_lo_ready, c + 1)
                w = split[:, slot, :, 0:kn * CW].rearrange("p s (k n) -> p s k n", n=CW)
                for m in range(2):
                    dst = acc[:, 2 * banks + m, :]
                    for k in range(kn):
                        if before is not None and m == 0:
                            before(k)
                        w_hi = w[:, 0, k, m * P:(m + 1) * P]
                        w_lo = w[:, 1, k, m * P:(m + 1) * P]
                        v_hi, v_lo = moving(k)
                        nc.tensor.matmul(dst, w_hi, v_lo, start=first and k == 0, stop=False)
                        nc.tensor.matmul(dst, w_hi, v_hi, start=False, stop=False)
                        mm = nc.tensor.matmul(dst, w_lo, v_hi, start=False, stop=final and k == kn - 1)
                        if between is not None and m == 0 and k == min(3, kn - 1):
                            between()
                mm.then_inc(chunk_done, 1)

            def from_mov(k):
                return mov[:, k, 0, :], mov[:, k, 1, :]

            pe.wait_ge(ident_ready, 1)
            pe.wait_ge(group_landed, 16)
            group_sb = z[:, 0:2, :].rearrange("p a (b e) -> p (a b) e", e=CW)
            for g in range(GROUPS):
                turn_unit(g, g % 2, [group_sb[:, 2 * g + ct, et * P:(et + 1) * P] for et in range(2) for ct in range(2)], P)
            pe.wait_ge(meta_landed, 16)
            for h in range(2):
                turn_unit(GROUPS + h, h, [z[0:N_META, 2, k * P:(k + 1) * P] for k in range(4 * h, 4 * h + 4)], N_META)

            for g in range(GROUPS):
                pe.wait_ge(turn_lo_ready, g + 1)
                pe.wait_ge(w_lo_ready, g + 1)
                if g >= 1:
                    pe.wait_ge(fold_a_staged, g)
                    pe.wait_ge(fold_b_staged, g)
                w = split[:, g % 2].rearrange("p s (e n) -> p s e n", e=2)
                gt = act_sb[:, KT + g].rearrange("p s (e c) -> p s e c", e=2)
                for ct in range(2):
                    for n in range(2):
                        for et in range(2):
                            for n3, (a, b) in enumerate(((0, 1), (0, 0), (1, 0))):
                                mm = nc.tensor.matmul(acc[:, 2 * ct + n, :], gt[:, a, et, ct * P:(ct + 1) * P],
                                                      w[:, b, et, n * TOK:(n + 1) * TOK],
                                                      start=et == 0 and n3 == 0, stop=et == 1 and n3 == 2)
                mm.then_inc(chunk_done, 1)
                turn_tile(0, g)

            def meta_products(i):
                pe.wait_ge(w_lo_ready, c_in(0, i) + 1)
                if i >= 2:
                    pe.wait_ge(meta_u_taken, i - 1)
                w = split[:, i % 2].rearrange("p s (k n) -> p s k n", n=CW)
                for m in range(2):
                    for k in range(KT):
                        for n3, (a, b) in enumerate(((0, 1), (0, 0), (1, 0))):
                            mm = nc.tensor.matmul(back[:, i % 2, m * H:(m + 1) * H], w[:, a, k, m * P:(m + 1) * P],
                                                  meta_t[:, k, b, :], start=k == 0 and n3 == 0,
                                                  stop=k == KT - 1 and n3 == 2)
                mm.then_inc(meta_u_done, 1)

            def mixer_block(b, first=False):
                pe.wait_ge(turn_lo_ready, turn_x(b) + 2 * TT)
                for i in range(PAIRS):
                    if first:
                        meta_products(i)
                    if i >= 2:
                        pe.wait_ge(u_staged, b * PAIRS + (i - 1))
                    elif first:
                        pe.wait_ge([fold_a_staged, fold_b_staged][i], GROUPS)
                    else:
                        pe.wait_ge(y_staged, b * PAIRS - 1 + i)
                    products(c_in(b, i), i % 2, i % 2, from_mov, KT,
                             between=(lambda: turn_back(b - 1, PAIRS - 1)) if i == 0 and not first else None)
                if first:
                    pe.wait_ge(meta_u_taken, PAIRS)
                for i in range(PAIRS):
                    if i < 2:
                        pe.wait_ge(u_staged, b * PAIRS + (PAIRS - 1 + i))
                    else:
                        pe.wait_ge(y_staged, b * PAIRS + (i - 1))

                    def d_is_ready(k):
                        if i == 0 and k % 2 == 0:
                            pe.wait_ge(d_lo_ready, b * PAIRS + (k // 2 + 1))

                    def others():
                        if i >= 1:
                            turn_back(b, i - 1)
                        turn_tile(b + 1, i)

                    products(c_mix(b, i), i % 2, i % 2, lambda k: (act_sb[:, k, 0, :], act_sb[:, k, 1, :]), KT,
                             before=d_is_ready, between=others)

            mixer_block(0, first=True)
            with pe.Fori(1, BLOCKS) as b:
                mixer_block(b)

            def ffn_block(b, last=False):
                s = b + BLOCKS
                pe.wait_ge(turn_lo_ready, turn_x(s) + 2 * TT)
                for up in range(2):
                    pe.wait_ge(y_staged, s * PAIRS - 1 + up)
                    products(c_gu(b, 0, up), up, up, from_mov, KT,
                             between=(lambda: turn_back(s - 1, PAIRS - 1)) if up == 0 else None)
                with pe.Fori(1, JF) as j:
                    pe.wait_ge(silu_done, b * JF + j)
                    products(c_gu(b, j, 0), 0, 0, from_mov, KT)
                    pe.wait_ge(a_ready, b * JF + j)
                    products(c_gu(b, j, 1), 1, 1, from_mov, KT)
                for p in range(PAIRS):
                    if p >= 2:
                        pe.wait_ge(y_staged, s * PAIRS + (p - 1))
                    else:
                        pe.wait_ge([silu_done, a_ready][p], b * JF + JF)
                    for t in range(DN):
                        def a_is_split(k):
                            if p == 0 and k % 2 == 0:
                                pe.wait_ge(a_lo_ready, b * JF + ((KT * t + k) // 2 + 1))

                        def others():
                            if t == 0 and p >= 1:
                                turn_back(s, p - 1)
                            if t == 1 and not last:
                                turn_tile(s + 1, p)

                        products(c_dn(b, p, t), (DN * p + t) % 2, p % 2,
                                 lambda k: (act_sb[:, KT * t + k, 0, :], act_sb[:, KT * t + k, 1, :]), KS[t],
                                 first=t == 0, final=t == DN - 1, before=a_is_split, between=others)

            with pe.Fori(0, BLOCKS - 1) as b:
                ffn_block(b)
            ffn_block(BLOCKS - 1, last=True)
            turn_back(2 * BLOCKS - 1, PAIRS - 1)

        @block.scalar
        def _(act):
            def split_hi(c, slot, kn=KT):
                if isinstance(c, int):
                    act.wait_ge(raw_landed[slot], 16 * (c // 2 + 1))
                else:
                    act.wait_ge(raw_landed[slot], (c - slot) * 8 + 16)
                if not (isinstance(c, int) and c < 2):
                    act.wait_ge(chunk_done, c - 1)
                nc.scalar.copy(split[:, slot, 0, 0:kn * CW], raw[:, slot, 0:kn * CW]).then_inc(w_hi_ready, 1)

            def turn_hi(unit, bank, dst, width=P):
                act.wait_ge(turn_done, unit + 1)
                src = turn[:, bank, 0:4 * width].rearrange("p (k n) -> p k n", k=4)
                nc.scalar.copy(dst, src).then_inc(turn_hi_ready, 1)

            def turn_tile_hi(b, i):
                for h in range(2):
                    turn_hi(turn_x(b) + (2 * i + h), h, mov[:, 4 * h:4 * h + 4, 0, i * P:(i + 1) * P])

            def stage_u(b, i):
                act.wait_ge(chunk_done, c_in(b, i) + 1)
                nc.scalar.copy(staged(), pair(i % 2)).then_inc(u_staged, 1)

            def stage_y(s, p, c):
                act.wait_ge(chunk_done, c + 1)
                nc.scalar.copy(staged(), pair(p % 2)).then_inc(y_staged, 1)

            def d_hi(b, i):
                act.wait_ge(d_ready, b * PAIRS + (i + 1))
                nc.scalar.copy(act_sb[:, 2 * i:2 * i + 2, 0, :], sums[1][:, :, H:]).then_inc(d_hi_ready, 1)

            for g in range(GROUPS):
                turn_hi(g, g % 2, act_sb[:, KT + g, 0, :].rearrange("p (k n) -> p k n", k=4))
            for h in range(2):
                turn_hi(GROUPS + h, h, meta_t[:, 4 * h:4 * h + 4, 0, :], N_META)
            for g in range(GROUPS):
                act.wait_ge(raw_scaled, 2 * g + 2)
                if g >= 1:
                    def stage_fold(gp):
                        act.wait_ge(chunk_done, gp + 1)
                        if gp >= 2:
                            act.wait_ge(fold_stored[gp % 2], 32)
                        nc.scalar.copy(fold_st[:, gp % 2, 0, :].rearrange("p (a n) -> p a n", a=2),
                                       pair(0)).then_inc(fold_a_staged, 1)
                if g >= 2:
                    stage_fold(g - 2)
                split_hi(g, g % 2)
                if g >= 2:
                    turn_tile_hi(0, g - 2)
            stage_fold(GROUPS - 2)
            split_hi(c_in(0, 0), 0)
            turn_tile_hi(0, GROUPS - 2)
            stage_fold(GROUPS - 1)
            turn_tile_hi(0, GROUPS - 1)
            split_hi(c_in(0, 1), 1)

            def mixer_block(b, first=False):
                for i in range(PAIRS):
                    if i == 0 and not first:
                        stage_y(b - 1, PAIRS - 1, c_mix(b - 1, PAIRS - 1))
                    if i >= 1:
                        if i == 1 and not first:
                            act.wait_ge(back_done, b * (2 * PAIRS))
                        stage_u(b, i - 1)
                    if not (first and i == 0):
                        split_hi(c_in(b, i + 1), (i + 1) % 2)
                    if i >= 1:
                        d_hi(b, i - 1)
                for i in range(PAIRS):
                    if i == 0:
                        stage_u(b, PAIRS - 1)
                        d_hi(b, PAIRS - 1)
                    else:
                        if i >= 2:
                            act.wait_ge(back_done, b * (2 * PAIRS) + 2 * (i - 1))
                        stage_y(b, i - 1, c_mix(b, i - 1))
                    split_hi(c_mix(b, i + 1), (i + 1) % 2)
                    turn_tile_hi(b + 1, i)

            mixer_block(0, first=True)
            with act.Fori(1, BLOCKS) as b:
                mixer_block(b)

            def silu(b, j):
                act.wait_ge(chunk_done, c_gu(b, j, 0) + 1)
                if not (isinstance(j, int) and j == 0):
                    act.wait_ge(a_lo_ready, b * JF + j)
                nc.scalar.activation(staged(), pair(0), ACT.Silu).then_inc(silu_done, 1)

            def a_hi(b, j):
                act.wait_ge(a_ready, b * JF + j + 1)
                nc.scalar.copy(act_sb[:, bass.ds(j * 2, 2), 0, :], staged()).then_inc(a_hi_ready, 1)

            def ffn_block(b, last=False):
                s = b + BLOCKS
                act.wait_ge(back_done, s * (2 * PAIRS) - 2)
                stage_y(s - 1, PAIRS - 1, c_gu(b, 0, 0) - 1)
                split_hi(c_gu(b, 0, 1), 1)
                act.wait_ge(back_done, s * (2 * PAIRS))
                silu(b, 0)
                split_hi(c_gu(b, 1, 0), 0)
                with act.Fori(1, JF) as j:
                    split_hi(c_gu(b, j, 1), 1)
                    a_hi(b, j - 1)
                    silu(b, j)
                    split_hi(c_gu(b, j + 1, 0), 0)
                for p in range(PAIRS):
                    for t in range(DN):
                        if t == 0 and p == 0:
                            a_hi(b, JF - 1)
                        if t == 0 and p >= 1:
                            if p == 1:
                                act.wait_ge(a_lo_ready, b * JF + JF)
                            else:
                                act.wait_ge(back_done, s * (2 * PAIRS) + 2 * (p - 1))
                            stage_y(s, p - 1, c_dn(b, p - 1, DN - 1))
                        n = DN * p + t + 1
                        if n < DN * PAIRS:
                            split_hi(c_dn(b, 0, n), n % 2, KS[n % DN])
                        elif not last:
                            split_hi(c_gu(b + 1, 0, 0), 0)
                        if t == 1 and not last:
                            turn_tile_hi(s + 1, p)

            with act.Fori(0, BLOCKS - 1) as b:
                ffn_block(b)
            ffn_block(BLOCKS - 1, last=True)
            act.wait_ge(back_done, 2 * BLOCKS * 2 * PAIRS - 2)
            stage_y(2 * BLOCKS - 1, PAIRS - 1, c_dn(BLOCKS - 1, PAIRS - 1, DN - 1))

        @block.vector
        def _(dve):
            def split_lo(c, slot, kn=KT):
                dve.wait_ge(w_hi_ready, c + 1)
                nc.vector.tensor_tensor(split[:, slot, 1, 0:kn * CW], raw[:, slot, 0:kn * CW],
                                        f32(split[:, slot, 0, 0:kn * CW]), ALU.subtract).then_inc(w_lo_ready, 1)

            def turn_lo(unit, bank, dst, hi, width=P):
                dve.wait_ge(turn_hi_ready, unit + 1)
                src = turn[:, bank, 0:4 * width].rearrange("p (k n) -> p k n", k=4)
                nc.vector.tensor_tensor(dst, src, f32(hi), ALU.subtract).then_inc(turn_lo_ready, 1)

            def turn_tile_lo(b, i):
                for h in range(2):
                    cols = slice(i * P, (i + 1) * P)
                    turn_lo(turn_x(b) + (2 * i + h), h, mov[:, 4 * h:4 * h + 4, 1, cols], mov[:, 4 * h:4 * h + 4, 0, cols])

            LINKS = [1 + int(math.log2(w)) if w > 2 else 1 for w in reversed(WINDOWS)]
            LINKS_BLOCK = sum(LINKS)

            def pool(b, i):
                w = WINDOWS[GROUPS - 1 - i]
                link = [b * LINKS_BLOCK + sum(LINKS[:i])]

                def linked(ins):
                    ins.then_inc(pool_link, 1)
                    link[0] = link[0] + 1
                    dve.wait_ge(pool_link, link[0])

                dve.wait_ge(u_staged, b * PAIRS + (i + 1))
                linked(nc.vector.tensor_copy(stage[:, :, 0:H], hist[:, 2 * i:2 * i + 2, :]))
                nc.vector.tensor_copy(hist[:, 2 * i:2 * i + 2, :], stage[:, :, TOK:TOK + H])
                if w == 2:
                    nc.vector.tensor_tensor(sums[1][:, :, H:], stage[:, :, H - 1:H + TOK - 1], stage[:, :, H:],
                                            ALU.subtract).then_inc(d_ready, 1)
                    return
                levels = int(math.log2(w))
                cur = stage
                for n in range(levels):
                    shift = 2 ** n
                    lo = H - (w - 2 * shift)
                    nxt = sums[(levels - 1 - n) % 2]
                    linked(nc.vector.tensor_tensor(nxt[:, :, lo:], cur[:, :, lo:],
                                                   cur[:, :, lo - shift:H + TOK - shift], ALU.add))
                    cur = nxt
                nc.vector.scalar_tensor_tensor(out=sums[1][:, :, H:], in0=stage[:, :, H:], scalar=-float(w),
                                               in1=cur[:, :, H:], op0=ALU.mult, op1=ALU.add).then_inc(d_ready, 1)

            def d_lo(b, i):
                dve.wait_ge(d_hi_ready, b * PAIRS + (i + 1))
                nc.vector.tensor_tensor(act_sb[:, 2 * i:2 * i + 2, 1, :], sums[1][:, :, H:],
                                        f32(act_sb[:, 2 * i:2 * i + 2, 0, :]), ALU.subtract).then_inc(d_lo_ready, 1)

            def add_rows(s, p):
                if p == 0:
                    dve.wait_ge(z_landed, s * 16 + 16)
                for m in range(2):
                    dve.wait_ge(back_done, s * (2 * PAIRS) + (2 * p + m + 1))
                    cols = z[:, :, p * CW + m * P:p * CW + (m + 1) * P]
                    nc.vector.scalar_tensor_tensor(out=cols, in0=cols, scalar=ALPHA,
                                                   in1=back[:, m, :].rearrange("p (j n) -> p j n", j=TT),
                                                   op0=ALU.mult, op1=ALU.add).then_inc(added, 1)
                dve.wait_ge(added, s * (2 * PAIRS) + (2 * p + 2))
                for j in range(TT):
                    nc.vector.bn_stats(stats[:, j, p, :], z[:, j, p * CW:(p + 1) * CW]).then_inc(stats_done, 1)

            def stats_are_done(s):
                dve.wait_ge(stats_done, s * (PAIRS * TT) + PAIRS * TT)

            def aggregate(s):
                for j in range(TT):
                    nc.vector.bn_aggr(mv[:, j, :], stats[:, j].rearrange("p a b -> p (a b)")).then_inc(aggr_done, 1)
                dve.wait_ge(aggr_done, s * TT + TT)
                nc.vector.tensor_scalar(var_eps[:], mv[:, :, 1], EPS, None, ALU.add).then_inc(var_ready, 1)

            def apply(s, j):
                if j == 0:
                    dve.wait_ge(rstd_ready, s + 1)
                nc.vector.scalar_tensor_tensor(out=z[:, j, :], in0=z[:, j, :], scalar=mv[:, j, 0:1], in1=gb[:, 0, :],
                                               op0=ALU.subtract, op1=ALU.mult).then_inc(centered, 1)
                dve.wait_ge(centered, s * TT + (j + 1))
                nc.vector.scalar_tensor_tensor(out=z[:, j, :], in0=z[:, j, :], scalar=rstd[:, j:j + 1], in1=gb[:, 1, :],
                                               op0=ALU.mult, op1=ALU.add).then_inc(ln_applied, 1)

            def scale_raw(g):
                dve.wait_ge(raw_landed[g % 2], 16 * (g // 2 + 1))
                for e in range(2):
                    half = raw[:, g % 2, e * D:(e + 1) * D]
                    nc.vector.tensor_scalar(half, half, scale_sb[:, 2 * g + e:2 * g + e + 1], 1.0 / WINDOWS[g],
                                            ALU.mult, ALU.mult).then_inc(raw_scaled, 1)

            def stage_fold(g):
                dve.wait_ge(chunk_done, g + 1)
                if g >= 2:
                    dve.wait_ge(fold_stored[g % 2], 32)
                nc.vector.tensor_copy(fold_st[:, g % 2, 1, :].rearrange("p (a n) -> p a n", a=2),
                                      pair(1)).then_inc(fold_b_staged, 1)

            dve.wait_ge(scale_landed, 16)
            for g in range(GROUPS):
                t = act_sb[:, KT + g]
                turn_lo(g, g % 2, t[:, 1, :].rearrange("p (k n) -> p k n", k=4), t[:, 0, :].rearrange("p (k n) -> p k n", k=4))
            for h in range(2):
                turn_lo(GROUPS + h, h, meta_t[:, 4 * h:4 * h + 4, 1, :], meta_t[:, 4 * h:4 * h + 4, 0, :], N_META)
            for g in range(GROUPS):
                scale_raw(g)
                if g >= 2:
                    stage_fold(g - 2)
                split_lo(g, g % 2)
                if g >= 2:
                    turn_tile_lo(0, g - 2)
            stage_fold(GROUPS - 2)
            split_lo(c_in(0, 0), 0)
            turn_tile_lo(0, GROUPS - 2)
            stage_fold(GROUPS - 1)
            turn_tile_lo(0, GROUPS - 1)
            split_lo(c_in(0, 1), 1)
            dve.wait_ge(gb_landed, 32)

            def take_meta(i):
                dve.wait_ge(meta_u_done, i + 1)
                nc.vector.tensor_copy(hist[:, 2 * i:2 * i + 2, :],
                                      back[:, i % 2, 0:2 * H].rearrange("p (m n) -> p m n", m=2)).then_inc(meta_u_taken, 1)

            def mixer_block(b, first=False):
                for i in range(PAIRS):
                    if first:
                        take_meta(i)
                        if i >= 1:
                            dve.wait_ge(meta_u_taken, i)
                    if i == 0 and not first:
                        add_rows(b - 1, PAIRS - 1)
                        stats_are_done(b - 1)
                    if first and i == 1:
                        for n in range(2):
                            dve.wait_ge(fold_stored[n], 16 * GROUPS)
                    if i >= 1:
                        pool(b, i - 1)
                    if not (first and i == 0):
                        split_lo(c_in(b, i + 1), (i + 1) % 2)
                    if i == 0 and not first:
                        aggregate(b - 1)
                    if i >= 1:
                        d_lo(b, i - 1)
                    if not first:
                        for j in ((0,), (), (1,), (2, 3))[i]:
                            apply(b - 1, j)
                for i in range(PAIRS):
                    if i == 0:
                        if first:
                            dve.wait_ge(meta_u_taken, PAIRS)
                        pool(b, PAIRS - 1)
                        d_lo(b, PAIRS - 1)
                    split_lo(c_mix(b, i + 1), (i + 1) % 2)
                    if i >= 1:
                        add_rows(b, i - 1)
                    turn_tile_lo(b + 1, i)

            mixer_block(0, first=True)
            with dve.Fori(1, BLOCKS) as b:
                mixer_block(b)

            def gated(b, j):
                dve.wait_ge(chunk_done, c_gu(b, j, 1) + 1)
                dve.wait_ge(silu_done, b * JF + j + 1)
                nc.vector.tensor_tensor(staged(), staged(), pair(1), ALU.mult).then_inc(a_ready, 1)

            def a_lo(b, j):
                dve.wait_ge(a_hi_ready, b * JF + j + 1)
                nc.vector.tensor_tensor(act_sb[:, bass.ds(j * 2, 2), 1, :], staged(),
                                        f32(act_sb[:, bass.ds(j * 2, 2), 0, :]), ALU.subtract).then_inc(a_lo_ready, 1)

            def ffn_block(b, last=False):
                s = b + BLOCKS
                add_rows(s - 1, PAIRS - 1)
                stats_are_done(s - 1)
                split_lo(c_gu(b, 0, 1), 1)
                aggregate(s - 1)
                apply(s - 1, 0)
                split_lo(c_gu(b, 1, 0), 0)

                def gate_up(j, tile=None):
                    gated(b, j - 1)
                    split_lo(c_gu(b, j, 1), 1)
                    a_lo(b, j - 1)
                    if tile is not None:
                        apply(s - 1, tile)
                    split_lo(c_gu(b, j + 1, 0), 0)

                for j in range(1, TT):
                    gate_up(j, j)
                dve.wait_ge(gb_landed, 64)
                with dve.Fori(TT, JF) as j:
                    gate_up(j)
                for p in range(PAIRS):
                    for t in range(DN):
                        n = DN * p + t + 1
                        if p == 0 and t == 0:
                            gated(b, JF - 1)
                        if n < DN * PAIRS:
                            split_lo(c_dn(b, 0, n), n % 2, KS[n % DN])
                        elif not last:
                            split_lo(c_gu(b + 1, 0, 0), 0)
                        if t == 0 and p == 0:
                            a_lo(b, JF - 1)
                        if t == 0 and p >= 1:
                            add_rows(s, p - 1)
                        if t == 1 and not last:
                            turn_tile_lo(s + 1, p)

            with dve.Fori(0, BLOCKS - 1) as b:
                ffn_block(b)
            ffn_block(BLOCKS - 1, last=True)
            add_rows(2 * BLOCKS - 1, PAIRS - 1)
            stats_are_done(2 * BLOCKS - 1)
            aggregate(2 * BLOCKS - 1)
            for j in range(TT):
                apply(2 * BLOCKS - 1, j)


def kernel(**inputs):
    import numpy as np
    import concourse.bacc as bacc
    from concourse import mybir as mb
    from concourse.bass_utils import run_bass_kernel_spmd

    seq, d = inputs["x"].shape[1:]
    names = ["x", "meta", "a_w_in", "a_w_group", "a_scale", "a_w_out", "ln_mix_g", "ln_mix_b",
             "ffn_w_gu", "ffn_w_down", "ln_ffn_g", "ln_ffn_b"]
    arrays = {}
    for name in names:
        a = np.asarray(inputs[name])
        arrays[name] = np.ascontiguousarray(a if name == "meta" else a[0])
    arrays["a_scale"] = np.ascontiguousarray(arrays["a_scale"].reshape(-1, P).T)
    nc = bacc.Bacc("TRN2", target_bir_lowering=False, num_devices=1)
    args = [nc.dram_tensor(n, arrays[n].shape, mb.dt.from_np(arrays[n].dtype), kind="ExternalInput").ap() for n in names]
    args.append(nc.dram_tensor("out", (seq, d), mb.dt.float32, kind="ExternalOutput").ap())
    args.append(nc.dram_tensor("fold_dram", (d, d), mb.dt.float32, kind="Internal").ap())
    args.append(nc.dram_tensor("h_dram", (seq, d), mb.dt.float32, kind="Internal").ap())
    trunk(nc, *args)
    r = run_bass_kernel_spmd(nc, [arrays], core_ids=[0])
    return r.results[0]["out"].reshape(1, seq, d)
```

```python
import math
from contextlib import ExitStack

import concourse.bass as bass
from concourse import mybir

F32 = mybir.dt.float32
F32R = mybir.dt.float32r
ALU = mybir.AluOpType
ACT = mybir.ActivationFunctionType

P = 128
TOK = 512
CW = 256
WINDOWS = (2, 4, 8, 16)
GROUPS = len(WINDOWS)
EPS = 1e-5
ALPHA = 2.0 ** 0.25
H = max(WINDOWS)


def trunk(nc, x, x_t, meta_t, w_in, w_group_t, scale, w_out, mix_g, mix_b, w_gu, w_down, ffn_g, ffn_b,
          out, fold_dram, h_dram):
    SEQ, D = x.shape
    N_META = meta_t.shape[2]
    FT = w_down.shape[2]
    JF = w_gu.shape[0]
    KT = D // P
    BLOCKS = SEQ // TOK
    TT = TOK // P
    PAIRS = D // CW
    HALVES = D // TOK
    KC = KT // 2
    MIXC = KT // KC
    DNC = -(-FT // KC)
    KS = [min(KC, FT - KC * t) for t in range(DNC)]
    CHUNK = KT * CW
    assert KT == 8 and PAIRS == GROUPS == TT == HALVES * MIXC and N_META == H and CHUNK == KC * TOK == 2 * D

    MIX0 = GROUPS
    FFN0 = MIX0 + 2 * PAIRS * BLOCKS
    DOWNS = HALVES * DNC
    PER_FFN = 2 * JF + DOWNS
    assert MIX0 % 2 == 0 and FFN0 % 2 == 0 and PER_FFN % 2 == 0

    def c_in(b, i):
        return b * (2 * PAIRS) + (MIX0 + i)

    def c_mix(b, i):
        return b * (2 * PAIRS) + (MIX0 + PAIRS + i)

    def c_gu(b, j, up):
        return b * PER_FFN + j * 2 + (FFN0 + up)

    def c_dn(b, n):
        return b * PER_FFN + (FFN0 + 2 * JF + n)

    OUT_BANK = [[4, 5, 0, 1], [2, 3, 4, 5]]
    ADDS = HALVES * TT

    x_rows = x.rearrange("(n p) d -> p n d", p=P)
    h_rows = h_dram.rearrange("(n p) d -> p n d", p=P)
    out_rows = out.rearrange("(n p) d -> p n d", p=P)

    with ExitStack() as ctx:
        def sb(name, shape, dt=F32):
            return ctx.enter_context(nc.sbuf_tensor(name, shape, dt))

        def sem(name):
            return ctx.enter_context(nc.semaphore(name))

        act_base = -(-nc.sbuf_base // 32) * 32
        act_sb = sb("act_sb", [P, FT, 2, TOK], F32R)
        assert nc.sbuf_base == act_base + FT * 2 * TOK * 4
        spare = act_base + (KT + 2 * GROUPS) * 2 * TOK * 4
        sums = [nc.alloc_sbuf_tensor_at(f"sums{n}", [P, 2, H + TOK], F32, offset=spare + n * 2 * (H + TOK) * 4)
                for n in range(2)]
        fold_st = nc.alloc_sbuf_tensor_at("fold_st", [P, 2, 2, D], F32, offset=spare)
        assert spare + 4 * D * 4 <= act_base + FT * 2 * TOK * 4
        mov = sb("mov", [P, KT, 2, TOK], F32R)
        split = sb("split", [P, 2, 2, CHUNK], F32R)
        raw = sb("raw", [P, 2, CHUNK])
        z = sb("z", [P, TT, D])
        nat = sb("nat", [P, 2, D])
        gb = sb("gb", [P, 2, D])
        stage = sb("stage", [P, 2, H + TOK])
        hist = sb("hist", [P, KT, H])
        meta_sb = sb("meta_sb", [P, KT, N_META])
        meta_s = sb("meta_s", [P, KT, 2, N_META], F32R)
        ident = sb("ident", [P, P])
        scale_sb = sb("scale_sb", [P, KT])
        stats = sb("stats", [P, TT, HALVES, 6])
        mv = sb("mv", [P, TT, 2])
        var_eps = sb("var_eps", [P, TT])
        rstd = sb("rstd", [P, TT])
        minus_half = sb("minus_half", [P, TT])

        acc = ctx.enter_context(nc.psum_tensor("acc", [P, 6, TOK], F32))
        turn = ctx.enter_context(nc.psum_tensor("turn", [P, 2, TOK], F32))

        raw_landed = [sem("raw_landed0"), sem("raw_landed1")]
        wout_landed = [[sem(f"wout_landed{n}{e}") for e in range(2)] for n in range(2)]
        nat_landed = [sem("nat_landed0"), sem("nat_landed1")]
        z_landed = sem("z_landed")
        group_landed = [sem("group_landed0"), sem("group_landed1")]
        meta_landed = sem("meta_landed")
        scale_landed = sem("scale_landed")
        gb_landed = sem("gb_landed")
        fold_stored = [sem("fold_stored0"), sem("fold_stored1")]
        rows_stored = sem("rows_stored")
        ident_zero = sem("ident_zero")
        ident_ready = sem("ident_ready")
        half_ready = sem("half_ready")
        group_hi_ready = sem("group_hi_ready")
        group_lo_ready = sem("group_lo_ready")
        meta_hi_ready = sem("meta_hi_ready")
        meta_lo_ready = sem("meta_lo_ready")
        wout_hi_ready = sem("wout_hi_ready")
        wout_lo_ready = sem("wout_lo_ready")
        w_hi_ready = sem("w_hi_ready")
        w_lo_ready = sem("w_lo_ready")
        chunk_done = sem("chunk_done")
        fold_done = sem("fold_done")
        fold_a_staged = sem("fold_a_staged")
        fold_b_staged = sem("fold_b_staged")
        x_hi_ready = sem("x_hi_ready")
        x_lo_ready = sem("x_lo_ready")
        turn_done = sem("turn_done")
        turn_hi_ready = sem("turn_hi_ready")
        turn_lo_ready = sem("turn_lo_ready")
        meta_u_done = sem("meta_u_done")
        meta_u_taken = sem("meta_u_taken")
        u_staged = sem("u_staged")
        pool_link = sem("pool_link")
        d_ready = sem("d_ready")
        d_hi_ready = sem("d_hi_ready")
        d_lo_ready = sem("d_lo_ready")
        out_done = sem("out_done")
        added = sem("added")
        silu_done = sem("silu_done")
        a_ready = sem("a_ready")
        a_hi_ready = sem("a_hi_ready")
        a_lo_ready = sem("a_lo_ready")
        stats_done = sem("stats_done")
        aggr_done = sem("aggr_done")
        var_ready = sem("var_ready")
        rstd_ready = sem("rstd_ready")
        centered = sem("centered")
        ln_applied = sem("ln_applied")

        block = ctx.enter_context(nc.Block())

        def pair(n):
            return acc[:, 2 * n:2 * n + 2, :]

        def staged():
            return stage[:, :, H:H + TOK]

        def f32(ap):
            return ap.bitcast(F32)

        def after_fold(c):
            return c - (GROUPS - 1)

        @block.sync
        def _(sp):
            def load_chunk(c, slot, src):
                if isinstance(c, int) and c < GROUPS + 2:
                    sp.wait_ge(wout_lo_ready, 2 * (c - 1))
                else:
                    sp.wait_ge(w_lo_ready, after_fold(c - 2))
                src = src.rearrange("p a b -> p (a b)") if len(src.shape) == 3 else src
                sp.dma_start(raw[:, slot, 0:src.shape[1]], src).then_inc(raw_landed[slot], 16)

            def load_wout(g):
                if g >= 2:
                    sp.wait_ge(wout_lo_ready, 2 * (g - 1))
                for e in range(2):
                    sp.dma_start(raw[:, g % 2, e * D:(e + 1) * D], w_out[g, :, e, :]).then_inc(wout_landed[g % 2][e], 16)

            def load_x(b, i):
                if not (isinstance(b, int) and b == 0 and i < 2):
                    sp.wait_ge(x_lo_ready, b * PAIRS + (i - 1))
                sp.dma_start(nat[:, i % 2, :], x_t[bass.ds(b, 1), :, 2 * i:2 * i + 2, :].rearrange("a p k t -> p (a k t)")
                             ).then_inc(nat_landed[i % 2], 16)

            def load_h(b, i):
                if isinstance(b, int) and b == 0 and i < 2:
                    sp.wait_ge(x_lo_ready, BLOCKS * PAIRS - 1 + i)
                else:
                    sp.wait_ge(turn_done, b * (2 * TT) + 2 * (i - 1))
                sp.dma_start(nat[:, i % 2, :], h_rows[:, bass.ds(b * TT + i, 1), :].rearrange("p a d -> p (a d)")
                             ).then_inc(nat_landed[i % 2], 16)

            def load_z(rows, s, b):
                if not (isinstance(s, int) and s == 0):
                    sp.wait_ge(rows_stored, s * (16 * TT))
                sp.dma_start(z[:], rows[:, bass.ds(b * TT, TT), :]).then_inc(z_landed, 16)

            def store_rows(rows, s, b, j):
                sp.wait_ge(ln_applied, s * TT + (j + 1))
                sp.dma_start(rows[:, bass.ds(b * TT + j, 1), :].rearrange("p a d -> p (a d)"),
                             z[:, j, :]).then_inc(rows_stored, 16)

            def store_fold(g):
                sp.wait_ge(fold_a_staged, g + 1)
                sp.wait_ge(fold_b_staged, g + 1)
                for ct in range(2):
                    k = 2 * (GROUPS - 1 - g) + ct
                    dst = fold_dram.rearrange("(n c) p k t -> c k p n t", n=HALVES)[k // KC, k % KC]
                    src = fold_st[:, g % 2, ct, :].rearrange("p (n t) -> p n t", n=HALVES)
                    sp.dma_start(dst, src).then_inc(fold_stored[g % 2], 16)

            def load_group(n):
                sp.dma_start(z[:, n, :], w_group_t[:, n * D:(n + 1) * D]).then_inc(group_landed[n], 16)

            load_group(0)
            sp.dma_start(scale_sb[:], scale).then_inc(scale_landed, 16)
            load_wout(0)
            load_wout(1)
            load_group(1)
            load_wout(2)
            load_x(0, 0)
            load_x(0, 1)
            load_wout(3)
            load_chunk(c_in(0, 0), 0, w_in[0])
            load_x(0, 2)
            load_x(0, 3)
            store_fold(0)
            sp.dma_start(meta_sb[:], meta_t).then_inc(meta_landed, 16)
            load_chunk(c_in(0, 1), 1, w_in[1])
            store_fold(1)
            for n, v in enumerate((mix_g, mix_b)):
                sp.dma_start(gb[:, n, :], v.partition_broadcast(P)).then_inc(gb_landed, 16)
            load_chunk(c_in(0, 2), 0, w_in[2])
            store_fold(2)
            store_fold(3)
            load_chunk(c_in(0, 3), 1, w_in[3])
            sp.wait_ge(group_lo_ready, 2)
            load_z(x_rows, 0, 0)
            for n in range(2):
                sp.wait_ge(fold_stored[n], 16 * GROUPS)

            def mixer_block(b, first=False, last=False):
                if not first:
                    for i in range(PAIRS):
                        load_chunk(c_in(b, i), i % 2, w_in[i])
                    store_rows(h_rows, b - 1, b - 1, 0)
                for i in range(PAIRS):
                    load_chunk(c_mix(b, i), i % 2, fold_dram[i])
                    if not first:
                        if i == 1:
                            store_rows(h_rows, b - 1, b - 1, 1)
                        if i == 2:
                            store_rows(h_rows, b - 1, b - 1, 2)
                            store_rows(h_rows, b - 1, b - 1, 3)
                            load_z(x_rows, b, b)
                    if not last:
                        load_x(b + 1, i)
                    elif i < 2:
                        load_h(0, i)

            mixer_block(0, first=True)
            with sp.Fori(1, BLOCKS - 1) as b:
                mixer_block(b)
            mixer_block(BLOCKS - 1, last=True)

            def gu_chunks(b, j):
                for up in range(2):
                    load_chunk(c_gu(b, j, up), up, w_gu[bass.ds(j, 1), up].rearrange("a p k n -> p (a k) n"))

            def ffn_block(b, first=False, last=False):
                rows, row_b = (h_rows, BLOCKS - 1) if first else (out_rows, b - 1)
                gu_chunks(b, 0)
                if first:
                    load_h(0, 2)
                    load_h(0, 3)
                for j in range(1, 1 + TT):
                    gu_chunks(b, j)
                    store_rows(rows, b + (BLOCKS - 1), row_b, j - 1)
                if first:
                    for n, v in enumerate((ffn_g, ffn_b)):
                        sp.dma_start(gb[:, n, :], v.partition_broadcast(P)).then_inc(gb_landed, 16)
                load_z(h_rows, b + BLOCKS, b)
                with sp.Fori(1 + TT, JF) as j:
                    gu_chunks(b, j)
                for n in range(DOWNS):
                    half, t = n // DNC, n % DNC
                    load_chunk(c_dn(b, n), n % 2, w_down[half, :, KC * t:KC * t + KS[t], :])
                    if n % (DOWNS // TT) == 1 and not last:
                        load_h(b + 1, n // (DOWNS // TT))

            ffn_block(0, first=True)
            with sp.Fori(1, BLOCKS - 1) as b:
                ffn_block(b)
            ffn_block(BLOCKS - 1, last=True)
            for j in range(TT):
                store_rows(out_rows, 2 * BLOCKS - 1, BLOCKS - 1, j)
            sp.wait_ge(rows_stored, 2 * BLOCKS * TT * 16)

        @block.gpsimd
        def _(pool):
            nc.gpsimd.memset(ident[:], 0.0).then_inc(ident_zero, 1)
            pool.wait_ge(ident_zero, 1)
            nc.gpsimd.affine_select(out=ident[:], in_=ident[:], compare_op=ALU.not_equal, fill=1.0, base=0,
                                    pattern=[[-1, P]], channel_multiplier=1).then_inc(ident_ready, 1)
            nc.gpsimd.memset(minus_half[:], -0.5).then_inc(half_ready, 1)
            pool.wait_ge(half_ready, 1)
            with pool.Fori(0, 2 * BLOCKS) as s:
                pool.wait_ge(var_ready, s + 1)
                nc.gpsimd.tensor_tensor(rstd[:], var_eps[:], minus_half[:], ALU.pow).then_inc(rstd_ready, 1)

        @block.tensor
        def _(pe):
            PARTS = ((0, 1), (0, 0), (1, 0))

            def chunk_is_split(c):
                pe.wait_ge(w_lo_ready, after_fold(c))

            def turn_tile(b, i):
                pe.wait_ge(nat_landed[i % 2], b * (16 * TT // 2) + 16 * (i // 2 + 1 + BLOCKS * PAIRS // 2))
                for h in range(2):
                    if not (isinstance(b, int) and b == 0 and i == 0):
                        pe.wait_ge(turn_lo_ready, b * (2 * TT) + (2 * i + h - 1))
                    for n in range(4):
                        k = 4 * h + n
                        mm = nc.tensor.transpose(turn[:, h, n * P:(n + 1) * P], nat[:, i % 2, k * P:(k + 1) * P], ident[:])
                    mm.then_inc(turn_done, 1)

            def hidden(c, slot, banks):
                chunk_is_split(c)
                w = split[:, slot].rearrange("p s (k n) -> p s k n", n=CW)
                for m in range(2):
                    for k in range(KT):
                        for n3, (a, v) in enumerate(PARTS):
                            mm = nc.tensor.matmul(acc[:, 2 * banks + m, :], w[:, a, k, m * P:(m + 1) * P],
                                                  mov[:, k, v, :], start=k == 0 and n3 == 0,
                                                  stop=k == KT - 1 and n3 == 2)
                mm.then_inc(chunk_done, 1)

            def outward(c, slot, half, k0, kn, first, final, bank_is_free, between=None):
                chunk_is_split(c)
                w = split[:, slot, :, 0:kn * TOK].rearrange("p s (k n) -> p s k n", n=TOK)
                for j in range(TT):
                    if first:
                        bank_is_free(half, j)
                    for k in range(kn):
                        for n3, (v, a) in enumerate(PARTS):
                            mm = nc.tensor.matmul(acc[:, OUT_BANK[half][j], :],
                                                  act_sb[:, k0 + k, v, j * P:(j + 1) * P], w[:, a, k, :],
                                                  start=first and k == 0 and n3 == 0,
                                                  stop=final and k == kn - 1 and n3 == 2)
                    if final and j < TT - 1:
                        mm.then_inc(out_done, 1)
                    if between is not None and j == 1:
                        between()
                mm.then_inc(chunk_done, 1)

            def fold_pair_free(q):
                g, ct = q // 2, q % 2
                pe.wait_ge([fold_a_staged, fold_b_staged][ct], g + 1)

            for g in range(GROUPS):
                if g % 2 == 0:
                    pe.wait_ge(group_lo_ready, g // 2 + 1)
                w = split[:, g % 2].rearrange("p s (e n) -> p s e n", e=2)
                gt = act_sb[:, KT + g].rearrange("p s (e c) -> p s e c", e=2)
                for ct in range(2):
                    q = 2 * g + ct
                    if q >= 3:
                        fold_pair_free(q - 3)
                    for e in range(2):
                        if ct == 0:
                            pe.wait_ge(wout_lo_ready, 2 * g + e + 1)
                        for n in range(HALVES):
                            for n3, (a, v) in enumerate(PARTS):
                                mm = nc.tensor.matmul(acc[:, 2 * (q % 3) + n, :], gt[:, a, e, ct * P:(ct + 1) * P],
                                                      w[:, v, e, n * TOK:(n + 1) * TOK],
                                                      start=e == 0 and n3 == 0, stop=e == 1 and n3 == 2)
                    mm.then_inc([fold_done, chunk_done][ct], 1)

            def meta_products(i):
                chunk_is_split(c_in(0, i))
                if i == 0:
                    pe.wait_ge(meta_lo_ready, 1)
                    pe.wait_ge(fold_b_staged, GROUPS - 1)
                if i >= 2:
                    pe.wait_ge(meta_u_taken, i - 1)
                w = split[:, i % 2].rearrange("p s (k n) -> p s k n", n=CW)
                for m in range(2):
                    for k in range(KT):
                        for n3, (a, v) in enumerate(PARTS):
                            mm = nc.tensor.matmul(acc[:, 4 + i % 2, m * H:(m + 1) * H], w[:, a, k, m * P:(m + 1) * P],
                                                  meta_s[:, k, v, :], start=k == 0 and n3 == 0,
                                                  stop=k == KT - 1 and n3 == 2)
                mm.then_inc(meta_u_done, 1)

            def mixer_block(b, first=False):
                pe.wait_ge(x_lo_ready, b * PAIRS + PAIRS)
                for i in range(PAIRS):
                    if first:
                        meta_products(i)
                    if i >= 2:
                        pe.wait_ge(u_staged, b * PAIRS + (i - 1))
                    elif first:
                        pe.wait_ge([fold_a_staged, fold_b_staged][i], GROUPS)
                    else:
                        pe.wait_ge(added, b * ADDS - TT + 2 * i)
                    hidden(c_in(b, i), i % 2, i % 2)

                def bank_is_free(half, j):
                    if half == 0 and j < 2 and first:
                        pe.wait_ge(meta_u_taken, PAIRS - 1 + j)
                    elif half == 0 and j < 2:
                        pe.wait_ge(added, b * ADDS - 1 + j)
                    elif half == 1 and j >= 2:
                        pe.wait_ge(added, b * ADDS + (j - 1))
                    else:
                        pe.wait_ge(u_staged, b * PAIRS + (PAIRS - 1 + half))

                for i in range(PAIRS):
                    half, t = i // MIXC, i % MIXC
                    if half == 0:
                        pe.wait_ge(d_lo_ready, b * PAIRS + KC // 2 * (t + 1))
                    outward(c_mix(b, i), i % 2, half, KC * t, KC, t == 0, t == MIXC - 1, bank_is_free)

            mixer_block(0, first=True)
            with pe.Fori(1, BLOCKS) as b:
                mixer_block(b)

            pe.wait_ge(ident_ready, 1)
            for i in range(TT):
                turn_tile(0, i)

            def ffn_block(b, last=False):
                s = b + BLOCKS
                pe.wait_ge(turn_lo_ready, b * (2 * TT) + 2 * TT)
                for up in range(2):
                    pe.wait_ge(added, s * ADDS - TT + 2 * up)
                    hidden(c_gu(b, 0, up), up, up)
                with pe.Fori(1, JF) as j:
                    pe.wait_ge(silu_done, b * JF + j)
                    hidden(c_gu(b, j, 0), 0, 0)
                    pe.wait_ge(a_ready, b * JF + j)
                    hidden(c_gu(b, j, 1), 1, 1)

                def bank_is_free(half, j):
                    if half == 0 and j < 2:
                        pe.wait_ge(added, s * ADDS - 1 + j)
                    elif half == 1 and j >= 2:
                        pe.wait_ge(added, s * ADDS + (j - 1))
                    elif j % 2 == 0:
                        pe.wait_ge([silu_done, a_ready][half], b * JF + JF)

                for n in range(DOWNS):
                    half, t = n // DNC, n % DNC
                    if half == 0:
                        pe.wait_ge(a_lo_ready, b * JF + (KC * t + KS[t]) // 2)
                    turns = n % (DOWNS // TT) == 1 and not last
                    outward(c_dn(b, n), n % 2, half, KC * t, KS[t], t == 0, t == DNC - 1, bank_is_free,
                            between=(lambda: turn_tile(b + 1, n // (DOWNS // TT))) if turns else None)

            with pe.Fori(0, BLOCKS - 1) as b:
                ffn_block(b)
            ffn_block(BLOCKS - 1, last=True)

        @block.scalar
        def _(act):
            def split_hi(c, slot, kn=CHUNK):
                act.wait_ge(raw_landed[slot], (c - slot) * 8 - 8 * (GROUPS - 2))
                act.wait_ge(chunk_done, c - 1)
                nc.scalar.copy(split[:, slot, 0, 0:kn], raw[:, slot, 0:kn]).then_inc(w_hi_ready, 1)

            def x_hi(b, i):
                act.wait_ge(nat_landed[i % 2], b * (8 * PAIRS) + 16 * (i // 2 + 1))
                nc.scalar.copy(mov[:, 2 * i:2 * i + 2, 0, :], nat[:, i % 2, :].rearrange("p (k t) -> p k t", k=2)
                               ).then_inc(x_hi_ready, 1)

            def turn_tile_hi(b, i):
                for h in range(2):
                    act.wait_ge(turn_done, b * (2 * TT) + (2 * i + h + 1))
                    nc.scalar.copy(mov[:, 4 * h:4 * h + 4, 0, i * P:(i + 1) * P],
                                   turn[:, h, :].rearrange("p (k n) -> p k n", k=4)).then_inc(turn_hi_ready, 1)

            def stage_u(b, i):
                act.wait_ge(chunk_done, c_in(b, i) + 1)
                nc.scalar.copy(staged(), pair(i % 2)).then_inc(u_staged, 1)

            def d_hi(b, i):
                act.wait_ge(d_ready, b * PAIRS + (i + 1))
                nc.scalar.mul(act_sb[:, 2 * i:2 * i + 2, 0, :], sums[1][:, :, H:], 1.0 / WINDOWS[GROUPS - 1 - i]
                              ).then_inc(d_hi_ready, 1)

            def group_hi(n):
                act.wait_ge(group_landed[n], 16)
                nc.scalar.copy(act_sb[:, KT + 2 * n:KT + 2 * n + 2, 0, :],
                               z[:, n, :].rearrange("p (g t) -> p g t", g=2)).then_inc(group_hi_ready, 1)

            def wout_hi(g):
                for e in range(2):
                    act.wait_ge(wout_landed[g % 2][e], 16 * (g // 2 + 1))
                    if g >= 2:
                        act.wait_ge(chunk_done, g - 1)
                    nc.scalar.mul(split[:, g % 2, 0, e * D:(e + 1) * D], raw[:, g % 2, e * D:(e + 1) * D],
                                  scale_sb[:, 2 * g + e:2 * g + e + 1]).then_inc(wout_hi_ready, 1)

            def stage_fold(g):
                act.wait_ge(fold_done, g + 1)
                if g >= 2:
                    act.wait_ge(fold_stored[g % 2], 32)
                nc.scalar.copy(fold_st[:, g % 2, 0, :].rearrange("p (a n) -> p a n", a=2),
                               pair(2 * g % 3)).then_inc(fold_a_staged, 1)

            group_hi(0)
            act.wait_ge(scale_landed, 16)
            wout_hi(0)
            wout_hi(1)
            group_hi(1)
            stage_fold(0)
            wout_hi(2)
            x_hi(0, 0)
            x_hi(0, 1)
            stage_fold(1)
            wout_hi(3)
            x_hi(0, 2)
            x_hi(0, 3)
            act.wait_ge(meta_landed, 16)
            nc.scalar.copy(meta_s[:, :, 0, :], meta_sb[:]).then_inc(meta_hi_ready, 1)
            stage_fold(2)
            split_hi(c_in(0, 0), 0)
            stage_fold(3)
            split_hi(c_in(0, 1), 1)

            def mixer_block(b, first=False):
                for i in range(PAIRS):
                    if i >= 1:
                        stage_u(b, i - 1)
                    if not (first and i == 0):
                        split_hi(c_in(b, i + 1), (i + 1) % 2)
                    if i >= 1:
                        d_hi(b, i - 1)
                for i in range(PAIRS):
                    if i == 0:
                        stage_u(b, PAIRS - 1)
                        d_hi(b, PAIRS - 1)
                    split_hi(c_mix(b, i + 1), (i + 1) % 2)
                    if not (isinstance(b, int) and b == BLOCKS - 1):
                        x_hi(b + 1, i)

            mixer_block(0, first=True)
            with act.Fori(1, BLOCKS - 1) as b:
                mixer_block(b)
            mixer_block(BLOCKS - 1)
            for i in range(TT):
                turn_tile_hi(0, i)

            def silu(b, j):
                act.wait_ge(chunk_done, c_gu(b, j, 0) + 1)
                if not (isinstance(j, int) and j == 0):
                    act.wait_ge(a_lo_ready, b * JF + j)
                nc.scalar.activation(staged(), pair(0), ACT.Silu).then_inc(silu_done, 1)

            def a_hi(b, j):
                act.wait_ge(a_ready, b * JF + j + 1)
                nc.scalar.copy(act_sb[:, bass.ds(j * 2, 2), 0, :], staged()).then_inc(a_hi_ready, 1)

            def ffn_block(b, last=False):
                split_hi(c_gu(b, 0, 1), 1)
                silu(b, 0)
                split_hi(c_gu(b, 1, 0), 0)
                with act.Fori(1, JF) as j:
                    split_hi(c_gu(b, j, 1), 1)
                    a_hi(b, j - 1)
                    silu(b, j)
                    split_hi(c_gu(b, j + 1, 0), 0)
                for n in range(DOWNS):
                    if n == 0:
                        a_hi(b, JF - 1)
                    if n + 1 < DOWNS:
                        split_hi(c_dn(b, n + 1), (n + 1) % 2, KS[(n + 1) % DNC] * TOK)
                    elif not last:
                        split_hi(c_gu(b + 1, 0, 0), 0)
                    if n % (DOWNS // TT) == 1 and not last:
                        turn_tile_hi(b + 1, n // (DOWNS // TT))

            with act.Fori(0, BLOCKS - 1) as b:
                ffn_block(b)
            ffn_block(BLOCKS - 1, last=True)

        @block.vector
        def _(dve):
            def split_lo(c, slot, kn=CHUNK):
                dve.wait_ge(w_hi_ready, after_fold(c))
                nc.vector.tensor_tensor(split[:, slot, 1, 0:kn], raw[:, slot, 0:kn],
                                        f32(split[:, slot, 0, 0:kn]), ALU.subtract).then_inc(w_lo_ready, 1)

            def x_lo(b, i):
                dve.wait_ge(x_hi_ready, b * PAIRS + (i + 1))
                nc.vector.tensor_tensor(mov[:, 2 * i:2 * i + 2, 1, :], nat[:, i % 2, :].rearrange("p (k t) -> p k t", k=2),
                                        f32(mov[:, 2 * i:2 * i + 2, 0, :]), ALU.subtract).then_inc(x_lo_ready, 1)

            def turn_tile_lo(b, i):
                for h in range(2):
                    dve.wait_ge(turn_hi_ready, b * (2 * TT) + (2 * i + h + 1))
                    hi, lo = (mov[:, 4 * h:4 * h + 4, n, i * P:(i + 1) * P] for n in range(2))
                    nc.vector.tensor_tensor(lo, turn[:, h, :].rearrange("p (k n) -> p k n", k=4), f32(hi),
                                            ALU.subtract).then_inc(turn_lo_ready, 1)

            LINKS = [1 + int(math.log2(w)) if w > 2 else 1 for w in reversed(WINDOWS)]
            LINKS_BLOCK = sum(LINKS)

            def pool(b, i):
                w = WINDOWS[GROUPS - 1 - i]
                link = [b * LINKS_BLOCK + sum(LINKS[:i])]

                def linked(ins):
                    ins.then_inc(pool_link, 1)
                    link[0] = link[0] + 1
                    dve.wait_ge(pool_link, link[0])

                dve.wait_ge(u_staged, b * PAIRS + (i + 1))
                linked(nc.vector.tensor_copy(stage[:, :, 0:H], hist[:, 2 * i:2 * i + 2, :]))
                nc.vector.tensor_copy(hist[:, 2 * i:2 * i + 2, :], stage[:, :, TOK:TOK + H])
                if w == 2:
                    nc.vector.tensor_tensor(sums[1][:, :, H:], stage[:, :, H - 1:H + TOK - 1], stage[:, :, H:],
                                            ALU.subtract).then_inc(d_ready, 1)
                    return
                levels = int(math.log2(w))
                cur = stage
                for n in range(levels):
                    shift = 2 ** n
                    lo = H - (w - 2 * shift)
                    nxt = sums[(levels - 1 - n) % 2]
                    linked(nc.vector.tensor_tensor(nxt[:, :, lo:], cur[:, :, lo:],
                                                   cur[:, :, lo - shift:H + TOK - shift], ALU.add))
                    cur = nxt
                nc.vector.scalar_tensor_tensor(out=sums[1][:, :, H:], in0=stage[:, :, H:], scalar=-float(w),
                                               in1=cur[:, :, H:], op0=ALU.mult, op1=ALU.add).then_inc(d_ready, 1)

            def d_lo(b, i):
                dve.wait_ge(d_hi_ready, b * PAIRS + (i + 1))
                nc.vector.scalar_tensor_tensor(out=act_sb[:, 2 * i:2 * i + 2, 1, :], in0=sums[1][:, :, H:],
                                               scalar=1.0 / WINDOWS[GROUPS - 1 - i],
                                               in1=f32(act_sb[:, 2 * i:2 * i + 2, 0, :]),
                                               op0=ALU.mult, op1=ALU.subtract).then_inc(d_lo_ready, 1)

            def add_rows(s, half, tiles, c):
                if half == 0 and 0 in tiles:
                    dve.wait_ge(z_landed, s * 16 + 16)
                cols = slice(half * TOK, (half + 1) * TOK)
                for j in tiles:
                    if j < TT - 1:
                        dve.wait_ge(out_done, s * (HALVES * (TT - 1)) + (half * (TT - 1) + j + 1))
                    else:
                        dve.wait_ge(chunk_done, c + 1)
                    nc.vector.scalar_tensor_tensor(out=z[:, j, cols], in0=z[:, j, cols], scalar=ALPHA,
                                                   in1=acc[:, OUT_BANK[half][j], :],
                                                   op0=ALU.mult, op1=ALU.add).then_inc(added, 1)
                dve.wait_ge(added, s * ADDS + (half * TT + tiles[-1] + 1))
                for j in tiles:
                    nc.vector.bn_stats(stats[:, j, half, :], z[:, j, cols]).then_inc(stats_done, 1)

            def stats_are_done(s):
                dve.wait_ge(stats_done, s * ADDS + ADDS)

            def aggregate(s):
                for j in range(TT):
                    nc.vector.bn_aggr(mv[:, j, :], stats[:, j].rearrange("p a b -> p (a b)")).then_inc(aggr_done, 1)
                dve.wait_ge(aggr_done, s * TT + TT)
                nc.vector.tensor_scalar(var_eps[:], mv[:, :, 1], EPS, None, ALU.add).then_inc(var_ready, 1)

            def apply(s, j):
                nc.vector.scalar_tensor_tensor(out=z[:, j, :], in0=z[:, j, :], scalar=mv[:, j, 0:1], in1=gb[:, 0, :],
                                               op0=ALU.subtract, op1=ALU.mult).then_inc(centered, 1)
                if j == 0:
                    dve.wait_ge(rstd_ready, s + 1)
                dve.wait_ge(centered, s * TT + (j + 1))
                nc.vector.scalar_tensor_tensor(out=z[:, j, :], in0=z[:, j, :], scalar=rstd[:, j:j + 1], in1=gb[:, 1, :],
                                               op0=ALU.mult, op1=ALU.add).then_inc(ln_applied, 1)

            def group_lo(n):
                dve.wait_ge(group_hi_ready, n + 1)
                t = act_sb[:, KT + 2 * n:KT + 2 * n + 2]
                nc.vector.tensor_tensor(t[:, :, 1, :], z[:, n, :].rearrange("p (g t) -> p g t", g=2), f32(t[:, :, 0, :]),
                                        ALU.subtract).then_inc(group_lo_ready, 1)

            def wout_lo(g):
                for e in range(2):
                    dve.wait_ge(wout_hi_ready, 2 * g + e + 1)
                    cols = slice(e * D, (e + 1) * D)
                    nc.vector.scalar_tensor_tensor(out=split[:, g % 2, 1, cols], in0=raw[:, g % 2, cols],
                                                   scalar=scale_sb[:, 2 * g + e:2 * g + e + 1],
                                                   in1=f32(split[:, g % 2, 0, cols]),
                                                   op0=ALU.mult, op1=ALU.subtract).then_inc(wout_lo_ready, 1)

            def stage_fold(g):
                dve.wait_ge(chunk_done, g + 1)
                if g >= 2:
                    dve.wait_ge(fold_stored[g % 2], 32)
                nc.vector.tensor_copy(fold_st[:, g % 2, 1, :].rearrange("p (a n) -> p a n", a=2),
                                      pair((2 * g + 1) % 3)).then_inc(fold_b_staged, 1)

            group_lo(0)
            dve.wait_ge(scale_landed, 16)
            wout_lo(0)
            wout_lo(1)
            group_lo(1)
            stage_fold(0)
            wout_lo(2)
            x_lo(0, 0)
            x_lo(0, 1)
            stage_fold(1)
            wout_lo(3)
            x_lo(0, 2)
            x_lo(0, 3)
            dve.wait_ge(meta_hi_ready, 1)
            nc.vector.tensor_tensor(meta_s[:, :, 1, :], meta_sb[:], f32(meta_s[:, :, 0, :]), ALU.subtract
                                    ).then_inc(meta_lo_ready, 1)
            stage_fold(2)
            split_lo(c_in(0, 0), 0)
            stage_fold(3)
            split_lo(c_in(0, 1), 1)
            dve.wait_ge(gb_landed, 32)

            def take_meta(i):
                dve.wait_ge(meta_u_done, i + 1)
                nc.vector.tensor_copy(hist[:, 2 * i:2 * i + 2, :],
                                      acc[:, 4 + i % 2, 0:2 * H].rearrange("p (m n) -> p m n", m=2)).then_inc(meta_u_taken, 1)

            def mixer_block(b, first=False, last=False):
                for i in range(PAIRS):
                    if first:
                        take_meta(i)
                        if i >= 1:
                            dve.wait_ge(meta_u_taken, i)
                    if i == 0 and not first:
                        add_rows(b - 1, 1, [TT - 1], c_mix(b - 1, PAIRS - 1))
                        stats_are_done(b - 1)
                    if first and i == 1:
                        for n in range(2):
                            dve.wait_ge(fold_stored[n], 16 * GROUPS)
                    if i >= 1:
                        pool(b, i - 1)
                    if not (first and i == 0):
                        split_lo(c_in(b, i + 1), (i + 1) % 2)
                    if i == 0 and not first:
                        aggregate(b - 1)
                    if i >= 1:
                        d_lo(b, i - 1)
                    if not first:
                        for j in ((0, 1), (), (2,), (3,))[i]:
                            apply(b - 1, j)
                for i in range(PAIRS):
                    if i == 0:
                        if first:
                            dve.wait_ge(meta_u_taken, PAIRS)
                        pool(b, PAIRS - 1)
                        d_lo(b, PAIRS - 1)
                    if i == MIXC:
                        add_rows(b, 0, list(range(TT)), c_mix(b, MIXC - 1))
                    split_lo(c_mix(b, i + 1), (i + 1) % 2)
                    if not last:
                        x_lo(b + 1, i)
                add_rows(b, 1, list(range(TT - 1)), None)

            mixer_block(0, first=True)
            with dve.Fori(1, BLOCKS - 1) as b:
                mixer_block(b)
            mixer_block(BLOCKS - 1, last=True)
            for i in range(TT):
                turn_tile_lo(0, i)

            def gated(b, j):
                dve.wait_ge(chunk_done, c_gu(b, j, 1) + 1)
                dve.wait_ge(silu_done, b * JF + j + 1)
                nc.vector.tensor_tensor(staged(), staged(), pair(1), ALU.mult).then_inc(a_ready, 1)

            def a_lo(b, j):
                dve.wait_ge(a_hi_ready, b * JF + j + 1)
                nc.vector.tensor_tensor(act_sb[:, bass.ds(j * 2, 2), 1, :], staged(),
                                        f32(act_sb[:, bass.ds(j * 2, 2), 0, :]), ALU.subtract).then_inc(a_lo_ready, 1)

            def ffn_block(b, last=False):
                s = b + BLOCKS
                add_rows(s - 1, 1, [TT - 1], c_gu(b, 0, 0) - 1)
                stats_are_done(s - 1)
                split_lo(c_gu(b, 0, 1), 1)
                aggregate(s - 1)
                apply(s - 1, 0)
                split_lo(c_gu(b, 1, 0), 0)

                def gate_up(j, tile=None):
                    gated(b, j - 1)
                    split_lo(c_gu(b, j, 1), 1)
                    a_lo(b, j - 1)
                    if tile is not None:
                        apply(s - 1, tile)
                    split_lo(c_gu(b, j + 1, 0), 0)

                for j in range(1, TT):
                    gate_up(j, j)
                dve.wait_ge(gb_landed, 64)
                with dve.Fori(TT, JF) as j:
                    gate_up(j)
                for n in range(DOWNS):
                    if n == 0:
                        gated(b, JF - 1)
                    if n == DNC:
                        add_rows(s, 0, list(range(TT)), c_dn(b, DNC - 1))
                    if n + 1 < DOWNS:
                        split_lo(c_dn(b, n + 1), (n + 1) % 2, KS[(n + 1) % DNC] * TOK)
                    elif not last:
                        split_lo(c_gu(b + 1, 0, 0), 0)
                    if n == 0:
                        a_lo(b, JF - 1)
                    if n % (DOWNS // TT) == 1 and not last:
                        turn_tile_lo(b + 1, n // (DOWNS // TT))
                add_rows(s, 1, list(range(TT - 1)), None)

            with dve.Fori(0, BLOCKS - 1) as b:
                ffn_block(b)
            ffn_block(BLOCKS - 1, last=True)
            s = 2 * BLOCKS - 1
            add_rows(s, 1, [TT - 1], c_dn(BLOCKS - 1, DOWNS - 1))
            stats_are_done(s)
            aggregate(s)
            for j in range(TT):
                apply(s, j)


def kernel(**inputs):
    import numpy as np
    import concourse.bacc as bacc
    from concourse import mybir as mb
    from concourse.bass_utils import run_bass_kernel_spmd

    def lay(a, shape, order):
        return np.ascontiguousarray(np.asarray(a).reshape(shape).transpose(order))

    seq, d = inputs["x"].shape[1:]
    n_meta, ff, kt, cp = inputs["meta"].shape[0], inputs["ffn_w_down"].shape[1], d // P, CW // P
    arrays = {
        "x": np.ascontiguousarray(inputs["x"][0]),
        "x_t": lay(inputs["x"], (seq // TOK, TOK, kt, P), (0, 3, 2, 1)),
        "meta_t": lay(inputs["meta"], (n_meta, kt, P), (2, 1, 0)),
        "w_in": lay(lay(inputs["a_w_in"], (kt, P, GROUPS, CW), (2, 1, 0, 3))[::-1], (GROUPS, P, kt, CW), (0, 1, 2, 3)),
        "w_group_t": lay(inputs["a_w_group"], (GROUPS, CW, cp, P), (3, 0, 2, 1)).reshape(P, -1),
        "scale": lay(inputs["a_scale"], (kt, P), (1, 0)),
        "w_out": lay(inputs["a_w_out"], (GROUPS, cp, P, d), (0, 2, 1, 3)),
        "mix_g": np.ascontiguousarray(inputs["ln_mix_g"][0]),
        "mix_b": np.ascontiguousarray(inputs["ln_mix_b"][0]),
        "w_gu": lay(inputs["ffn_w_gu"], (kt, P, 2, ff // CW, CW), (3, 2, 1, 0, 4)),
        "w_down": lay(inputs["ffn_w_down"], (ff // P, P, d // TOK, TOK), (2, 1, 0, 3)),
        "ffn_g": np.ascontiguousarray(inputs["ln_ffn_g"][0]),
        "ffn_b": np.ascontiguousarray(inputs["ln_ffn_b"][0]),
    }
    nc = bacc.Bacc("TRN2", target_bir_lowering=False, num_devices=1)
    f32 = mb.dt.float32
    args = [nc.dram_tensor(n, a.shape, mb.dt.from_np(a.dtype), kind="ExternalInput").ap() for n, a in arrays.items()]
    args.append(nc.dram_tensor("out", (seq, d), f32, kind="ExternalOutput").ap())
    args.append(nc.dram_tensor("fold_dram", (GROUPS, P, kt // 2, TOK), f32, kind="Internal").ap())
    args.append(nc.dram_tensor("h_dram", (seq, d), f32, kind="Internal").ap())
    trunk(nc, *args)
    r = run_bass_kernel_spmd(nc, [arrays], core_ids=[0])
    return r.results[0]["out"].reshape(1, seq, d)
```

```python
import math
from contextlib import ExitStack

import concourse.bass as bass
from concourse import mybir

F32 = mybir.dt.float32
F32R = mybir.dt.float32r
ALU = mybir.AluOpType
ACT = mybir.ActivationFunctionType

P = 128
TOK = 512
CW = 256
WINDOWS = (2, 4, 8, 16)
GROUPS = len(WINDOWS)
EPS = 1e-5
ALPHA = 2.0 ** 0.25
LO_AT = 32
H = max(WINDOWS)


def trunk(nc, x, x_t, meta_t, w_in, w_group_t, scale, w_out, mix_g, mix_b, w_gu, w_down, ffn_g, ffn_b,
          out, fold_dram, h_dram):
    SEQ, D = x.shape
    N_META = meta_t.shape[2]
    FT = w_down.shape[2]
    JF = w_gu.shape[0]
    KT = D // P
    BLOCKS = SEQ // TOK
    TT = TOK // P
    PAIRS = D // CW
    HALVES = D // TOK
    KC = KT // 2
    MIXC = KT // KC
    DNC = -(-FT // KC)
    KS = [min(KC, FT - KC * t) for t in range(DNC)]
    CHUNK = KT * CW
    assert KT == 8 and PAIRS == GROUPS == TT == HALVES * MIXC and N_META == H and CHUNK == KC * TOK == 2 * D

    MIX0 = GROUPS
    FFN0 = MIX0 + 2 * PAIRS * BLOCKS
    DOWNS = HALVES * DNC
    PER_FFN = 2 * JF + DOWNS
    assert MIX0 % 2 == 0 and FFN0 % 2 == 0 and PER_FFN % 2 == 0

    def c_in(b, i):
        return b * (2 * PAIRS) + (MIX0 + i)

    def c_mix(b, i):
        return b * (2 * PAIRS) + (MIX0 + PAIRS + i)

    def c_gu(b, j, up):
        return b * PER_FFN + j * 2 + (FFN0 + up)

    def c_dn(b, n):
        return b * PER_FFN + (FFN0 + 2 * JF + n)

    OUT_BANK = [[4, 5, 0, 1], [2, 3, 4, 5]]
    ADDS = HALVES * TT

    x_rows = x.rearrange("(n p) d -> p n d", p=P)
    h_rows = h_dram.rearrange("(n p) d -> p n d", p=P)
    out_rows = out.rearrange("(n p) d -> p n d", p=P)

    with ExitStack() as ctx:
        def sb(name, shape, dt=F32):
            return ctx.enter_context(nc.sbuf_tensor(name, shape, dt))

        def sem(name):
            return ctx.enter_context(nc.semaphore(name))

        act_base = -(-nc.sbuf_base // 32) * 32
        act_sb = sb("act_sb", [P, FT, 2, TOK], F32R)
        assert nc.sbuf_base == act_base + FT * 2 * TOK * 4
        spare = act_base + (KT + 2 * GROUPS) * 2 * TOK * 4
        sums = [nc.alloc_sbuf_tensor_at(f"sums{n}", [P, 2, H + TOK], F32, offset=spare + n * 2 * (H + TOK) * 4)
                for n in range(2)]
        fold_st = nc.alloc_sbuf_tensor_at("fold_st", [P, 2, 2, D], F32, offset=spare)
        assert spare + 4 * D * 4 <= act_base + FT * 2 * TOK * 4
        mov = sb("mov", [P, KT, 2, TOK], F32R)
        split = sb("split", [P, 2, 2, CHUNK], F32R)
        raw = sb("raw", [P, 2, CHUNK])
        z = sb("z", [P, TT, D])
        nat = sb("nat", [P, 2, D])
        gb = sb("gb", [P, 2, D])
        stage = sb("stage", [P, 2, H + TOK])
        hist = sb("hist", [P, KT, H])
        meta_sb = sb("meta_sb", [P, KT, N_META])
        meta_s = act_sb[:, KT + GROUPS].rearrange("p s t -> p (s t)").rearrange("p (k m) -> p k m", m=P)
        meta_rows = sb("meta_rows", [2 * LO_AT, CW])
        ident = sb("ident", [P, P])
        scale_sb = sb("scale_sb", [P, KT])
        stats = sb("stats", [P, TT, HALVES, 6])
        mv = sb("mv", [P, TT, 2])
        var_eps = sb("var_eps", [P, TT])
        rstd = sb("rstd", [P, TT])
        minus_half = sb("minus_half", [P, TT])

        acc = ctx.enter_context(nc.psum_tensor("acc", [P, 6, TOK], F32))
        turn = ctx.enter_context(nc.psum_tensor("turn", [P, 2, TOK], F32))

        raw_landed = [sem("raw_landed0"), sem("raw_landed1")]
        wout0_landed = [sem(f"wout0_landed{n}") for n in range(4)]
        wout_landed = [[sem(f"wout_landed{n}{e}") for e in range(2)] for n in range(2)]
        nat_landed = [sem("nat_landed0"), sem("nat_landed1")]
        z_landed = sem("z_landed")
        group_landed = [sem("group_landed0"), sem("group_landed1")]
        meta_landed = sem("meta_landed")
        scale_landed = sem("scale_landed")
        gb_landed = sem("gb_landed")
        fold_stored = [sem("fold_stored0"), sem("fold_stored1")]
        rows_stored = sem("rows_stored")
        ident_zero = sem("ident_zero")
        ident_ready = sem("ident_ready")
        half_ready = sem("half_ready")
        group_hi_ready = sem("group_hi_ready")
        group_lo_ready = sem("group_lo_ready")
        meta_zero = sem("meta_zero")
        meta_hi_ready = sem("meta_hi_ready")
        meta_lo_ready = sem("meta_lo_ready")
        wout_hi_ready = sem("wout_hi_ready")
        wout_lo_ready = sem("wout_lo_ready")
        w_hi_ready = sem("w_hi_ready")
        w_lo_ready = sem("w_lo_ready")
        chunk_done = sem("chunk_done")
        fold_done = sem("fold_done")
        fold_a_staged = sem("fold_a_staged")
        fold_b_staged = sem("fold_b_staged")
        x_hi_ready = sem("x_hi_ready")
        x_lo_ready = sem("x_lo_ready")
        turn_done = sem("turn_done")
        turn_hi_ready = sem("turn_hi_ready")
        turn_lo_ready = sem("turn_lo_ready")
        meta_rows_done = sem("meta_rows_done")
        meta_rows_staged = sem("meta_rows_staged")
        meta_u_done = sem("meta_u_done")
        meta_u_taken = sem("meta_u_taken")
        u_staged = sem("u_staged")
        pool_link = sem("pool_link")
        d_ready = sem("d_ready")
        d_hi_ready = sem("d_hi_ready")
        d_lo_ready = sem("d_lo_ready")
        out_done = sem("out_done")
        added = sem("added")
        silu_done = sem("silu_done")
        a_ready = sem("a_ready")
        a_hi_ready = sem("a_hi_ready")
        a_lo_ready = sem("a_lo_ready")
        stats_done = sem("stats_done")
        aggr_done = sem("aggr_done")
        var_ready = sem("var_ready")
        rstd_ready = sem("rstd_ready")
        centered = sem("centered")
        ln_applied = sem("ln_applied")

        group_sb = z[:, 0:2, :].rearrange("p a d -> p (a d)")
        WOUT_PIECES = [[(e, slice(n * TOK, (n + 1) * TOK)) for e in range(2) for n in range(HALVES)]]
        WOUT_PIECES += [[(e, slice(0, D)) for e in range(2)] for _ in range(1, GROUPS)]

        def wout_before(g):
            return sum(len(pieces) for pieces in WOUT_PIECES[:g])

        GROUP_PIECE = [slice(0, TOK), slice(TOK, GROUPS * TOK)]

        block = ctx.enter_context(nc.Block())

        def pair(n):
            return acc[:, 2 * n:2 * n + 2, :]

        def staged():
            return stage[:, :, H:H + TOK]

        def f32(ap):
            return ap.bitcast(F32)

        def after_fold(c):
            return c - (GROUPS - 1)

        @block.sync
        def _(sp):
            def load_chunk(c, slot, src):
                if isinstance(c, int) and c < GROUPS + 2:
                    sp.wait_ge(wout_lo_ready, wout_before(c - 1))
                else:
                    sp.wait_ge(w_lo_ready, after_fold(c - 2))
                src = src.rearrange("p a b -> p (a b)") if len(src.shape) == 3 else src
                sp.dma_start(raw[:, slot, 0:src.shape[1]], src).then_inc(raw_landed[slot], 16)

            def load_wout(g):
                if g >= 2:
                    sp.wait_ge(wout_lo_ready, wout_before(g - 1))
                for n, (e, cols) in enumerate(WOUT_PIECES[g]):
                    landed = wout0_landed[n] if g == 0 else wout_landed[g % 2][e]
                    sp.dma_start(raw[:, g % 2, e * D:(e + 1) * D][:, cols], w_out[g, :, e, cols]).then_inc(landed, 16)

            def load_x(b, i):
                if not (isinstance(b, int) and b == 0 and i < 2):
                    sp.wait_ge(x_lo_ready, b * PAIRS + (i - 1))
                sp.dma_start(nat[:, i % 2, :], x_t[bass.ds(b, 1), :, 2 * i:2 * i + 2, :].rearrange("a p k t -> p (a k t)")
                             ).then_inc(nat_landed[i % 2], 16)

            def load_h(b, i):
                if isinstance(b, int) and b == 0 and i < 2:
                    sp.wait_ge(x_lo_ready, BLOCKS * PAIRS - 1 + i)
                else:
                    sp.wait_ge(turn_done, b * (2 * TT) + 2 * (i - 1))
                sp.dma_start(nat[:, i % 2, :], h_rows[:, bass.ds(b * TT + i, 1), :].rearrange("p a d -> p (a d)")
                             ).then_inc(nat_landed[i % 2], 16)

            def load_z(rows, s, b):
                if not (isinstance(s, int) and s == 0):
                    sp.wait_ge(rows_stored, s * (16 * TT))
                sp.dma_start(z[:], rows[:, bass.ds(b * TT, TT), :]).then_inc(z_landed, 16)

            def store_rows(rows, s, b, j):
                sp.wait_ge(ln_applied, s * TT + (j + 1))
                sp.dma_start(rows[:, bass.ds(b * TT + j, 1), :].rearrange("p a d -> p (a d)"),
                             z[:, j, :]).then_inc(rows_stored, 16)

            def store_fold(g):
                sp.wait_ge(fold_a_staged, g + 1)
                sp.wait_ge(fold_b_staged, g + 1)
                for ct in range(2):
                    k = 2 * (GROUPS - 1 - g) + ct
                    dst = fold_dram.rearrange("(n c) p k t -> c k p n t", n=HALVES)[k // KC, k % KC]
                    src = fold_st[:, g % 2, ct, :].rearrange("p (n t) -> p n t", n=HALVES)
                    sp.dma_start(dst, src).then_inc(fold_stored[g % 2], 16)

            def load_group(n):
                cols = GROUP_PIECE[n]
                sp.dma_start(group_sb[:, cols], w_group_t[:, cols]).then_inc(group_landed[n], 16)

            load_group(0)
            sp.dma_start(scale_sb[:], scale).then_inc(scale_landed, 16)
            load_wout(0)
            load_group(1)
            load_wout(1)
            sp.dma_start(meta_sb[:], meta_t).then_inc(meta_landed, 16)
            load_wout(2)
            load_wout(3)
            load_x(0, 0)
            load_x(0, 1)
            store_fold(0)
            load_chunk(c_in(0, 0), 0, w_in[0])
            load_x(0, 2)
            load_x(0, 3)
            store_fold(1)
            load_chunk(c_in(0, 1), 1, w_in[1])
            for n, v in enumerate((mix_g, mix_b)):
                sp.dma_start(gb[:, n, :], v.partition_broadcast(P)).then_inc(gb_landed, 16)
            load_chunk(c_in(0, 2), 0, w_in[2])
            store_fold(2)
            store_fold(3)
            load_chunk(c_in(0, 3), 1, w_in[3])
            sp.wait_ge(group_lo_ready, 2)
            load_z(x_rows, 0, 0)
            for n in range(2):
                sp.wait_ge(fold_stored[n], 16 * GROUPS)

            def mixer_block(b, first=False, last=False):
                if not first:
                    for i in range(PAIRS):
                        load_chunk(c_in(b, i), i % 2, w_in[i])
                    store_rows(h_rows, b - 1, b - 1, 0)
                for i in range(PAIRS):
                    load_chunk(c_mix(b, i), i % 2, fold_dram[i])
                    if not first:
                        if i == 1:
                            store_rows(h_rows, b - 1, b - 1, 1)
                        if i == 2:
                            store_rows(h_rows, b - 1, b - 1, 2)
                            store_rows(h_rows, b - 1, b - 1, 3)
                            load_z(x_rows, b, b)
                    if not last:
                        load_x(b + 1, i)
                    else:
                        load_h(0, i)

            mixer_block(0, first=True)
            with sp.Fori(1, BLOCKS - 1) as b:
                mixer_block(b)
            mixer_block(BLOCKS - 1, last=True)

            def gu_chunks(b, j):
                for up in range(2):
                    load_chunk(c_gu(b, j, up), up, w_gu[bass.ds(j, 1), up].rearrange("a p k n -> p (a k) n"))

            def ffn_block(b, first=False, last=False):
                rows, row_b = (h_rows, BLOCKS - 1) if first else (out_rows, b - 1)
                gu_chunks(b, 0)
                for j in range(1, 1 + TT):
                    gu_chunks(b, j)
                    store_rows(rows, b + (BLOCKS - 1), row_b, j - 1)
                if first:
                    for n, v in enumerate((ffn_g, ffn_b)):
                        sp.dma_start(gb[:, n, :], v.partition_broadcast(P)).then_inc(gb_landed, 16)
                load_z(h_rows, b + BLOCKS, b)
                with sp.Fori(1 + TT, JF) as j:
                    gu_chunks(b, j)
                for n in range(DOWNS):
                    half, t = n // DNC, n % DNC
                    load_chunk(c_dn(b, n), n % 2, w_down[half, :, KC * t:KC * t + KS[t], :])
                    if n % (DOWNS // TT) == 1 and not last:
                        load_h(b + 1, n // (DOWNS // TT))

            ffn_block(0, first=True)
            with sp.Fori(1, BLOCKS - 1) as b:
                ffn_block(b)
            ffn_block(BLOCKS - 1, last=True)
            for j in range(TT):
                store_rows(out_rows, 2 * BLOCKS - 1, BLOCKS - 1, j)
            sp.wait_ge(rows_stored, 2 * BLOCKS * TT * 16)

        @block.gpsimd
        def _(pool):
            nc.gpsimd.memset(ident[:], 0.0).then_inc(ident_zero, 1)
            pool.wait_ge(ident_zero, 1)
            nc.gpsimd.affine_select(out=ident[:], in_=ident[:], compare_op=ALU.not_equal, fill=1.0, base=0,
                                    pattern=[[-1, P]], channel_multiplier=1).then_inc(ident_ready, 1)
            nc.gpsimd.memset(minus_half[:], -0.5).then_inc(half_ready, 1)
            pool.wait_ge(half_ready, 1)
            with pool.Fori(0, 2 * BLOCKS - 1) as s:
                pool.wait_ge(var_ready, s + 1)
                nc.gpsimd.tensor_tensor(rstd[:], var_eps[:], minus_half[:], ALU.pow).then_inc(rstd_ready, 1)
            for j in range(TT):
                pool.wait_ge(var_ready, 2 * BLOCKS + j)
                nc.gpsimd.tensor_tensor(rstd[:, j:j + 1], var_eps[:, j:j + 1], minus_half[:, j:j + 1], ALU.pow
                                        ).then_inc(rstd_ready, 1)

        @block.tensor
        def _(pe):
            PARTS = ((0, 1), (0, 0), (1, 0))

            def chunk_is_split(c):
                pe.wait_ge(w_lo_ready, after_fold(c))

            def turn_tile(b, i):
                pe.wait_ge(nat_landed[i % 2], b * (16 * TT // 2) + 16 * (i // 2 + 1 + BLOCKS * PAIRS // 2))
                for h in range(2):
                    if not (isinstance(b, int) and b == 0 and i == 0):
                        pe.wait_ge(turn_lo_ready, b * (2 * TT) + (2 * i + h - 1))
                    for n in range(4):
                        k = 4 * h + n
                        mm = nc.tensor.transpose(turn[:, h, n * P:(n + 1) * P], nat[:, i % 2, k * P:(k + 1) * P], ident[:])
                    mm.then_inc(turn_done, 1)

            def hidden(c, slot, banks, before=None):
                chunk_is_split(c)
                w = split[:, slot].rearrange("p s (k n) -> p s k n", n=CW)
                for m in range(2):
                    for k in range(KT):
                        if before is not None and m == 0:
                            before(k)
                        for n3, (a, v) in enumerate(PARTS):
                            mm = nc.tensor.matmul(acc[:, 2 * banks + m, :], w[:, a, k, m * P:(m + 1) * P],
                                                  mov[:, k, v, :], start=k == 0 and n3 == 0,
                                                  stop=k == KT - 1 and n3 == 2)
                mm.then_inc(chunk_done, 1)

            def outward(c, slot, half, k0, kn, first, final, bank_is_free, between=None):
                chunk_is_split(c)
                w = split[:, slot, :, 0:kn * TOK].rearrange("p s (k n) -> p s k n", n=TOK)
                for j in range(TT):
                    if first:
                        bank_is_free(half, j)
                    for k in range(kn):
                        for n3, (v, a) in enumerate(PARTS):
                            mm = nc.tensor.matmul(acc[:, OUT_BANK[half][j], :],
                                                  act_sb[:, k0 + k, v, j * P:(j + 1) * P], w[:, a, k, :],
                                                  start=first and k == 0 and n3 == 0,
                                                  stop=final and k == kn - 1 and n3 == 2)
                    if final and j < TT - 1:
                        mm.then_inc(out_done, 1)
                    if between is not None and j == 1:
                        between()
                mm.then_inc(chunk_done, 1)

            def fold_pair_free(q):
                g, ct = q // 2, q % 2
                pe.wait_ge([fold_a_staged, fold_b_staged][ct], g + 1)

            for g in range(GROUPS):
                if g < 2:
                    pe.wait_ge(group_lo_ready, g + 1)
                w = split[:, g % 2].rearrange("p s (e n) -> p s e n", e=2)
                gt = act_sb[:, KT + g].rearrange("p s (e c) -> p s e c", e=2)
                for ct in range(2):
                    q = 2 * g + ct
                    if q >= 3:
                        fold_pair_free(q - 3)
                    for e in range(2):
                        for n in range(HALVES):
                            if ct == 0 and g == 0:
                                pe.wait_ge(wout_lo_ready, HALVES * e + n + 1)
                            elif ct == 0 and n == 0:
                                pe.wait_ge(wout_lo_ready, wout_before(g) + e + 1)
                            for n3, (a, v) in enumerate(PARTS):
                                mm = nc.tensor.matmul(acc[:, 2 * (q % 3) + n, :], gt[:, a, e, ct * P:(ct + 1) * P],
                                                      w[:, v, e, n * TOK:(n + 1) * TOK],
                                                      start=e == 0 and n3 == 0, stop=e == 1 and n3 == 2)
                    mm.then_inc([fold_done, chunk_done][ct], 1)

            def meta_products(i):
                chunk_is_split(c_in(0, i))
                if i == 0:
                    pe.wait_ge(meta_lo_ready, 1)
                    pe.wait_ge(fold_b_staged, GROUPS - 1)
                w = split[:, i % 2].rearrange("p s (k n) -> p s k n", n=CW)
                for k in range(KT):
                    for a in range(2):
                        mm = nc.tensor.matmul(acc[:, 4, 0:CW], meta_s[:, k, :], w[:, a, k, :],
                                              start=k == 0 and a == 0, stop=k == KT - 1 and a == 1)
                mm.then_inc(meta_rows_done, 1)

            def meta_features(i):
                pe.wait_ge(meta_rows_staged, i + 1)
                if i == 0:
                    pe.wait_ge(ident_ready, 1)
                else:
                    pe.wait_ge(meta_u_taken, i)
                for m in range(2):
                    for v in range(2):
                        mm = nc.tensor.matmul(acc[:, 5, m * H:(m + 1) * H], meta_rows[:, m * P:(m + 1) * P],
                                              ident[0:2 * LO_AT, v * LO_AT:v * LO_AT + N_META],
                                              start=v == 0, stop=v == 1)
                mm.then_inc(meta_u_done, 1)

            def mixer_block(b, first=False, last=False):
                def x_is_split(k):
                    if k % 2 == 0:
                        pe.wait_ge(x_lo_ready, k // 2 + 1)

                if not first:
                    pe.wait_ge(x_lo_ready, b * PAIRS + PAIRS)
                for i in range(PAIRS):
                    if first:
                        meta_products(i)
                    if i >= 2:
                        pe.wait_ge(u_staged, b * PAIRS + (i - 1))
                    elif first:
                        pe.wait_ge([fold_a_staged, fold_b_staged][i], GROUPS)
                    else:
                        pe.wait_ge(added, b * ADDS - TT + 2 * i)
                    hidden(c_in(b, i), i % 2, i % 2, x_is_split if first and i == 0 else None)
                    if first:
                        meta_features(i)

                def bank_is_free(half, j):
                    if half == 0 and j < 2 and first:
                        pe.wait_ge([meta_rows_staged, meta_u_taken][j], PAIRS)
                    elif half == 0 and j < 2:
                        pe.wait_ge(added, b * ADDS - 1 + j)
                    elif half == 1 and j >= 2:
                        pe.wait_ge(added, b * ADDS + (j - 1))
                    else:
                        pe.wait_ge(u_staged, b * PAIRS + (PAIRS - 1 + half))

                for i in range(PAIRS):
                    half, t = i // MIXC, i % MIXC
                    if half == 0:
                        pe.wait_ge(d_lo_ready, b * PAIRS + KC // 2 * (t + 1))
                    outward(c_mix(b, i), i % 2, half, KC * t, KC, t == 0, t == MIXC - 1, bank_is_free,
                            between=(lambda: turn_tile(0, i)) if last else None)

            mixer_block(0, first=True)
            with pe.Fori(1, BLOCKS - 1) as b:
                mixer_block(b)
            mixer_block(BLOCKS - 1, last=True)

            def ffn_block(b, last=False):
                s = b + BLOCKS
                pe.wait_ge(turn_lo_ready, b * (2 * TT) + 2 * TT)
                for up in range(2):
                    pe.wait_ge(added, s * ADDS - TT + 2 * up)
                    hidden(c_gu(b, 0, up), up, up)
                with pe.Fori(1, JF) as j:
                    pe.wait_ge(silu_done, b * JF + j)
                    hidden(c_gu(b, j, 0), 0, 0)
                    pe.wait_ge(a_ready, b * JF + j)
                    hidden(c_gu(b, j, 1), 1, 1)

                def bank_is_free(half, j):
                    if half == 0 and j < 2:
                        pe.wait_ge(added, s * ADDS - 1 + j)
                    elif half == 1 and j >= 2:
                        pe.wait_ge(added, s * ADDS + (j - 1))
                    elif j % 2 == 0:
                        pe.wait_ge([silu_done, a_ready][half], b * JF + JF)

                for n in range(DOWNS - 2 * last):
                    half, t = n // DNC, n % DNC
                    if half == 0:
                        pe.wait_ge(a_lo_ready, b * JF + (KC * t + KS[t]) // 2)
                    turns = n % (DOWNS // TT) == 1 and not last
                    outward(c_dn(b, n), n % 2, half, KC * t, KS[t], t == 0, t == DNC - 1, bank_is_free,
                            between=(lambda: turn_tile(b + 1, n // (DOWNS // TT))) if turns else None)

            with pe.Fori(0, BLOCKS - 1) as b:
                ffn_block(b)
            ffn_block(BLOCKS - 1, last=True)
            for j in range(TT):
                for t in range(DNC - 2, DNC):
                    c = c_dn(BLOCKS - 1, DOWNS - DNC + t)
                    if j == 0:
                        chunk_is_split(c)
                    w = split[:, c % 2, :, 0:KS[t] * TOK].rearrange("p s (k n) -> p s k n", n=TOK)
                    for k in range(KS[t]):
                        for n3, (v, a) in enumerate(PARTS):
                            mm = nc.tensor.matmul(acc[:, OUT_BANK[1][j], :],
                                                  act_sb[:, KC * t + k, v, j * P:(j + 1) * P], w[:, a, k, :],
                                                  start=False, stop=t == DNC - 1 and k == KS[t] - 1 and n3 == 2)
                    if j == TT - 1:
                        mm.then_inc(chunk_done, 1)
                if j < TT - 1:
                    mm.then_inc(out_done, 1)

        @block.scalar
        def _(act):
            def split_hi(c, slot, kn=CHUNK):
                act.wait_ge(raw_landed[slot], (c - slot) * 8 - 8 * (GROUPS - 2))
                act.wait_ge(chunk_done, c - 1)
                nc.scalar.copy(split[:, slot, 0, 0:kn], raw[:, slot, 0:kn]).then_inc(w_hi_ready, 1)

            def x_hi(b, i):
                act.wait_ge(nat_landed[i % 2], b * (8 * PAIRS) + 16 * (i // 2 + 1))
                nc.scalar.copy(mov[:, 2 * i:2 * i + 2, 0, :], nat[:, i % 2, :].rearrange("p (k t) -> p k t", k=2)
                               ).then_inc(x_hi_ready, 1)

            def turn_tile_hi(b, i):
                for h in range(2):
                    act.wait_ge(turn_done, b * (2 * TT) + (2 * i + h + 1))
                    nc.scalar.copy(mov[:, 4 * h:4 * h + 4, 0, i * P:(i + 1) * P],
                                   turn[:, h, :].rearrange("p (k n) -> p k n", k=4)).then_inc(turn_hi_ready, 1)

            def stage_u(b, i):
                act.wait_ge(chunk_done, c_in(b, i) + 1)
                nc.scalar.copy(staged(), pair(i % 2)).then_inc(u_staged, 1)

            def d_hi(b, i):
                act.wait_ge(d_ready, b * PAIRS + (i + 1))
                nc.scalar.mul(act_sb[:, 2 * i:2 * i + 2, 0, :], sums[1][:, :, H:], 1.0 / WINDOWS[GROUPS - 1 - i]
                              ).then_inc(d_hi_ready, 1)

            def group_hi(n):
                act.wait_ge(group_landed[n], 16)
                tiles = slice(KT, KT + 1) if n == 0 else slice(KT + 1, KT + GROUPS)
                nc.scalar.copy(act_sb[:, tiles, 0, :],
                               group_sb[:, GROUP_PIECE[n]].rearrange("p (g t) -> p g t", t=TOK)).then_inc(group_hi_ready, 1)

            def wout_hi(g):
                for n, (e, cols) in enumerate(WOUT_PIECES[g]):
                    if g == 0:
                        act.wait_ge(wout0_landed[n], 16)
                    else:
                        act.wait_ge(wout_landed[g % 2][e], 16 * (g // 2 + g % 2))
                    if g >= 2:
                        act.wait_ge(chunk_done, g - 1)
                    nc.scalar.mul(split[:, g % 2, 0, e * D:(e + 1) * D][:, cols], raw[:, g % 2, e * D:(e + 1) * D][:, cols],
                                  scale_sb[:, 2 * g + e:2 * g + e + 1]).then_inc(wout_hi_ready, 1)

            def stage_fold(g):
                act.wait_ge(fold_done, g + 1)
                if g >= 2:
                    act.wait_ge(fold_stored[g % 2], 32)
                nc.scalar.copy(fold_st[:, g % 2, 0, :].rearrange("p (a n) -> p a n", a=2),
                               pair(2 * g % 3)).then_inc(fold_a_staged, 1)

            group_hi(0)
            act.wait_ge(scale_landed, 16)
            wout_hi(0)
            group_hi(1)
            wout_hi(1)
            act.wait_ge(meta_landed, 16)
            act.wait_ge(meta_zero, 1)
            nc.scalar.copy(meta_s[:, :, 0:N_META], meta_sb[:]).then_inc(meta_hi_ready, 1)
            stage_fold(0)
            wout_hi(2)
            stage_fold(1)
            wout_hi(3)
            x_hi(0, 0)
            x_hi(0, 1)
            stage_fold(2)
            split_hi(c_in(0, 0), 0)
            x_hi(0, 2)
            x_hi(0, 3)
            stage_fold(3)
            split_hi(c_in(0, 1), 1)

            def stage_meta(i):
                act.wait_ge(meta_rows_done, i + 1)
                if i >= 1:
                    act.wait_ge(meta_u_done, i)
                nc.scalar.copy(meta_rows[:], acc[0:2 * LO_AT, 4, 0:CW]).then_inc(meta_rows_staged, 1)

            def mixer_block(b, first=False, last=False):
                for i in range(PAIRS):
                    if i >= 1:
                        stage_u(b, i - 1)
                    if first:
                        stage_meta(i)
                    if not (first and i == 0):
                        split_hi(c_in(b, i + 1), (i + 1) % 2)
                    if i >= 1:
                        d_hi(b, i - 1)
                for i in range(PAIRS):
                    if i == 0:
                        stage_u(b, PAIRS - 1)
                        d_hi(b, PAIRS - 1)
                    split_hi(c_mix(b, i + 1), (i + 1) % 2)
                    if last:
                        turn_tile_hi(0, i)
                    else:
                        x_hi(b + 1, i)

            mixer_block(0, first=True)
            with act.Fori(1, BLOCKS - 1) as b:
                mixer_block(b)
            mixer_block(BLOCKS - 1, last=True)

            def silu(b, j):
                act.wait_ge(chunk_done, c_gu(b, j, 0) + 1)
                if not (isinstance(j, int) and j == 0):
                    act.wait_ge(a_lo_ready, b * JF + j)
                nc.scalar.activation(staged(), pair(0), ACT.Silu).then_inc(silu_done, 1)

            def a_hi(b, j):
                act.wait_ge(a_ready, b * JF + j + 1)
                nc.scalar.copy(act_sb[:, bass.ds(j * 2, 2), 0, :], staged()).then_inc(a_hi_ready, 1)

            def ffn_block(b, last=False):
                split_hi(c_gu(b, 0, 1), 1)
                silu(b, 0)
                split_hi(c_gu(b, 1, 0), 0)
                with act.Fori(1, JF) as j:
                    split_hi(c_gu(b, j, 1), 1)
                    a_hi(b, j - 1)
                    silu(b, j)
                    split_hi(c_gu(b, j + 1, 0), 0)
                for n in range(DOWNS):
                    if n == 0:
                        a_hi(b, JF - 1)
                    if n + 1 < DOWNS:
                        split_hi(c_dn(b, n + 1), (n + 1) % 2, KS[(n + 1) % DNC] * TOK)
                    elif not last:
                        split_hi(c_gu(b + 1, 0, 0), 0)
                    if n % (DOWNS // TT) == 1 and not last:
                        turn_tile_hi(b + 1, n // (DOWNS // TT))

            with act.Fori(0, BLOCKS - 1) as b:
                ffn_block(b)
            ffn_block(BLOCKS - 1, last=True)

        @block.vector
        def _(dve):
            def split_lo(c, slot, kn=CHUNK):
                dve.wait_ge(w_hi_ready, after_fold(c))
                nc.vector.tensor_tensor(split[:, slot, 1, 0:kn], raw[:, slot, 0:kn],
                                        f32(split[:, slot, 0, 0:kn]), ALU.subtract).then_inc(w_lo_ready, 1)

            def x_lo(b, i):
                dve.wait_ge(x_hi_ready, b * PAIRS + (i + 1))
                nc.vector.tensor_tensor(mov[:, 2 * i:2 * i + 2, 1, :], nat[:, i % 2, :].rearrange("p (k t) -> p k t", k=2),
                                        f32(mov[:, 2 * i:2 * i + 2, 0, :]), ALU.subtract).then_inc(x_lo_ready, 1)

            def turn_tile_lo(b, i):
                for h in range(2):
                    dve.wait_ge(turn_hi_ready, b * (2 * TT) + (2 * i + h + 1))
                    hi, lo = (mov[:, 4 * h:4 * h + 4, n, i * P:(i + 1) * P] for n in range(2))
                    nc.vector.tensor_tensor(lo, turn[:, h, :].rearrange("p (k n) -> p k n", k=4), f32(hi),
                                            ALU.subtract).then_inc(turn_lo_ready, 1)

            LINKS = [1 + int(math.log2(w)) if w > 2 else 1 for w in reversed(WINDOWS)]
            LINKS_BLOCK = sum(LINKS)

            def pool(b, i):
                w = WINDOWS[GROUPS - 1 - i]
                link = [b * LINKS_BLOCK + sum(LINKS[:i])]

                def linked(ins):
                    ins.then_inc(pool_link, 1)
                    link[0] = link[0] + 1
                    dve.wait_ge(pool_link, link[0])

                dve.wait_ge(u_staged, b * PAIRS + (i + 1))
                linked(nc.vector.tensor_copy(stage[:, :, 0:H], hist[:, 2 * i:2 * i + 2, :]))
                nc.vector.tensor_copy(hist[:, 2 * i:2 * i + 2, :], stage[:, :, TOK:TOK + H])
                if w == 2:
                    nc.vector.tensor_tensor(sums[1][:, :, H:], stage[:, :, H - 1:H + TOK - 1], stage[:, :, H:],
                                            ALU.subtract).then_inc(d_ready, 1)
                    return
                levels = int(math.log2(w))
                cur = stage
                for n in range(levels):
                    shift = 2 ** n
                    lo = H - (w - 2 * shift)
                    nxt = sums[(levels - 1 - n) % 2]
                    linked(nc.vector.tensor_tensor(nxt[:, :, lo:], cur[:, :, lo:],
                                                   cur[:, :, lo - shift:H + TOK - shift], ALU.add))
                    cur = nxt
                nc.vector.scalar_tensor_tensor(out=sums[1][:, :, H:], in0=stage[:, :, H:], scalar=-float(w),
                                               in1=cur[:, :, H:], op0=ALU.mult, op1=ALU.add).then_inc(d_ready, 1)

            def d_lo(b, i):
                dve.wait_ge(d_hi_ready, b * PAIRS + (i + 1))
                nc.vector.scalar_tensor_tensor(out=act_sb[:, 2 * i:2 * i + 2, 1, :], in0=sums[1][:, :, H:],
                                               scalar=1.0 / WINDOWS[GROUPS - 1 - i],
                                               in1=f32(act_sb[:, 2 * i:2 * i + 2, 0, :]),
                                               op0=ALU.mult, op1=ALU.subtract).then_inc(d_lo_ready, 1)

            def add_rows(s, half, tiles, c):
                if half == 0 and 0 in tiles:
                    dve.wait_ge(z_landed, s * 16 + 16)
                cols = slice(half * TOK, (half + 1) * TOK)
                for j in tiles:
                    if j < TT - 1:
                        dve.wait_ge(out_done, s * (HALVES * (TT - 1)) + (half * (TT - 1) + j + 1))
                    else:
                        dve.wait_ge(chunk_done, c + 1)
                    nc.vector.scalar_tensor_tensor(out=z[:, j, cols], in0=z[:, j, cols], scalar=ALPHA,
                                                   in1=acc[:, OUT_BANK[half][j], :],
                                                   op0=ALU.mult, op1=ALU.add).then_inc(added, 1)
                dve.wait_ge(added, s * ADDS + (half * TT + tiles[-1] + 1))
                for j in tiles:
                    nc.vector.bn_stats(stats[:, j, half, :], z[:, j, cols]).then_inc(stats_done, 1)

            def stats_are_done(s):
                dve.wait_ge(stats_done, s * ADDS + ADDS)

            def aggregate(s):
                for j in range(TT):
                    nc.vector.bn_aggr(mv[:, j, :], stats[:, j].rearrange("p a b -> p (a b)")).then_inc(aggr_done, 1)
                dve.wait_ge(aggr_done, s * TT + TT)
                nc.vector.tensor_scalar(var_eps[:], mv[:, :, 1], EPS, None, ALU.add).then_inc(var_ready, 1)

            def apply(s, j, rstd_count=None):
                nc.vector.scalar_tensor_tensor(out=z[:, j, :], in0=z[:, j, :], scalar=mv[:, j, 0:1], in1=gb[:, 0, :],
                                               op0=ALU.subtract, op1=ALU.mult).then_inc(centered, 1)
                if j == 0 or rstd_count is not None:
                    dve.wait_ge(rstd_ready, rstd_count or s + 1)
                dve.wait_ge(centered, s * TT + (j + 1))
                nc.vector.scalar_tensor_tensor(out=z[:, j, :], in0=z[:, j, :], scalar=rstd[:, j:j + 1], in1=gb[:, 1, :],
                                               op0=ALU.mult, op1=ALU.add).then_inc(ln_applied, 1)

            def group_lo(n):
                dve.wait_ge(group_hi_ready, n + 1)
                t = act_sb[:, KT:KT + 1] if n == 0 else act_sb[:, KT + 1:KT + GROUPS]
                nc.vector.tensor_tensor(t[:, :, 1, :], group_sb[:, GROUP_PIECE[n]].rearrange("p (g t) -> p g t", t=TOK),
                                        f32(t[:, :, 0, :]),
                                        ALU.subtract).then_inc(group_lo_ready, 1)

            def wout_lo(g):
                for n, (e, part) in enumerate(WOUT_PIECES[g]):
                    dve.wait_ge(wout_hi_ready, wout_before(g) + n + 1)
                    cols = slice(e * D + part.start, e * D + part.stop)
                    nc.vector.scalar_tensor_tensor(out=split[:, g % 2, 1, cols], in0=raw[:, g % 2, cols],
                                                   scalar=scale_sb[:, 2 * g + e:2 * g + e + 1],
                                                   in1=f32(split[:, g % 2, 0, cols]),
                                                   op0=ALU.mult, op1=ALU.subtract).then_inc(wout_lo_ready, 1)

            def stage_fold(g):
                dve.wait_ge(chunk_done, g + 1)
                if g >= 2:
                    dve.wait_ge(fold_stored[g % 2], 32)
                nc.vector.tensor_copy(fold_st[:, g % 2, 1, :].rearrange("p (a n) -> p a n", a=2),
                                      pair((2 * g + 1) % 3)).then_inc(fold_b_staged, 1)

            nc.vector.memset(f32(meta_s), 0.0).then_inc(meta_zero, 1)
            group_lo(0)
            dve.wait_ge(scale_landed, 16)
            wout_lo(0)
            group_lo(1)
            wout_lo(1)
            dve.wait_ge(meta_hi_ready, 1)
            nc.vector.tensor_tensor(meta_s[:, :, LO_AT:LO_AT + N_META], meta_sb[:], f32(meta_s[:, :, 0:N_META]),
                                    ALU.subtract).then_inc(meta_lo_ready, 1)
            stage_fold(0)
            wout_lo(2)
            stage_fold(1)
            wout_lo(3)
            x_lo(0, 0)
            x_lo(0, 1)
            stage_fold(2)
            split_lo(c_in(0, 0), 0)
            x_lo(0, 2)
            x_lo(0, 3)
            stage_fold(3)
            split_lo(c_in(0, 1), 1)
            dve.wait_ge(gb_landed, 32)

            def take_meta(i):
                dve.wait_ge(meta_u_done, i + 1)
                nc.vector.tensor_copy(hist[:, 2 * i:2 * i + 2, :],
                                      acc[:, 5, 0:2 * H].rearrange("p (m n) -> p m n", m=2)).then_inc(meta_u_taken, 1)

            def mixer_block(b, first=False, last=False):
                for i in range(PAIRS):
                    if first and i >= 1:
                        take_meta(i - 1)
                        dve.wait_ge(meta_u_taken, i)
                    if i == 0 and not first:
                        add_rows(b - 1, 1, [TT - 1], c_mix(b - 1, PAIRS - 1))
                        stats_are_done(b - 1)
                    if first and i == 1:
                        for n in range(2):
                            dve.wait_ge(fold_stored[n], 16 * GROUPS)
                    if i >= 1:
                        pool(b, i - 1)
                    if not (first and i == 0):
                        split_lo(c_in(b, i + 1), (i + 1) % 2)
                    if i == 0 and not first:
                        aggregate(b - 1)
                    if i >= 1:
                        d_lo(b, i - 1)
                    if not first:
                        for j in ((0, 1), (), (2,), (3,))[i]:
                            apply(b - 1, j)
                for i in range(PAIRS):
                    if i == 0:
                        if first:
                            take_meta(PAIRS - 1)
                            dve.wait_ge(meta_u_taken, PAIRS)
                        pool(b, PAIRS - 1)
                        d_lo(b, PAIRS - 1)
                    if i == MIXC:
                        add_rows(b, 0, list(range(TT)), c_mix(b, MIXC - 1))
                    split_lo(c_mix(b, i + 1), (i + 1) % 2)
                    if last:
                        turn_tile_lo(0, i)
                    else:
                        x_lo(b + 1, i)
                add_rows(b, 1, list(range(TT - 1)), None)

            mixer_block(0, first=True)
            with dve.Fori(1, BLOCKS - 1) as b:
                mixer_block(b)
            mixer_block(BLOCKS - 1, last=True)

            def gated(b, j):
                dve.wait_ge(chunk_done, c_gu(b, j, 1) + 1)
                dve.wait_ge(silu_done, b * JF + j + 1)
                nc.vector.tensor_tensor(staged(), staged(), pair(1), ALU.mult).then_inc(a_ready, 1)

            def a_lo(b, j):
                dve.wait_ge(a_hi_ready, b * JF + j + 1)
                nc.vector.tensor_tensor(act_sb[:, bass.ds(j * 2, 2), 1, :], staged(),
                                        f32(act_sb[:, bass.ds(j * 2, 2), 0, :]), ALU.subtract).then_inc(a_lo_ready, 1)

            def ffn_block(b, last=False):
                s = b + BLOCKS
                add_rows(s - 1, 1, [TT - 1], c_gu(b, 0, 0) - 1)
                stats_are_done(s - 1)
                split_lo(c_gu(b, 0, 1), 1)
                aggregate(s - 1)
                apply(s - 1, 0)
                split_lo(c_gu(b, 1, 0), 0)

                def gate_up(j, tile=None):
                    gated(b, j - 1)
                    split_lo(c_gu(b, j, 1), 1)
                    a_lo(b, j - 1)
                    if tile is not None:
                        apply(s - 1, tile)
                    split_lo(c_gu(b, j + 1, 0), 0)

                for j in range(1, TT):
                    gate_up(j, j)
                dve.wait_ge(gb_landed, 64)
                with dve.Fori(TT, JF) as j:
                    gate_up(j)
                for n in range(DOWNS):
                    if n == 0:
                        gated(b, JF - 1)
                    if n == DNC:
                        add_rows(s, 0, list(range(TT)), c_dn(b, DNC - 1))
                    if n + 1 < DOWNS:
                        split_lo(c_dn(b, n + 1), (n + 1) % 2, KS[(n + 1) % DNC] * TOK)
                    elif not last:
                        split_lo(c_gu(b + 1, 0, 0), 0)
                    if n == 0:
                        a_lo(b, JF - 1)
                    if n % (DOWNS // TT) == 1 and not last:
                        turn_tile_lo(b + 1, n // (DOWNS // TT))
                if not last:
                    add_rows(s, 1, list(range(TT - 1)), None)

            with dve.Fori(0, BLOCKS - 1) as b:
                ffn_block(b)
            ffn_block(BLOCKS - 1, last=True)
            s = 2 * BLOCKS - 1
            for j in range(TT):
                add_rows(s, 1, [j], c_dn(BLOCKS - 1, DOWNS - 1))
                dve.wait_ge(stats_done, s * ADDS + TT + j + 1)
                nc.vector.bn_aggr(mv[:, j, :], stats[:, j].rearrange("p a b -> p (a b)")).then_inc(aggr_done, 1)
                dve.wait_ge(aggr_done, s * TT + j + 1)
                nc.vector.tensor_scalar(var_eps[:, j:j + 1], mv[:, j, 1:2], EPS, None, ALU.add).then_inc(var_ready, 1)
                apply(s, j, s + j + 1)


def kernel(**inputs):
    import numpy as np
    import concourse.bacc as bacc
    from concourse import mybir as mb
    from concourse.bass_utils import run_bass_kernel_spmd

    def lay(a, shape, order):
        return np.ascontiguousarray(np.asarray(a).reshape(shape).transpose(order))

    seq, d = inputs["x"].shape[1:]
    n_meta, ff, kt, cp = inputs["meta"].shape[0], inputs["ffn_w_down"].shape[1], d // P, CW // P
    arrays = {
        "x": np.ascontiguousarray(inputs["x"][0]),
        "x_t": lay(inputs["x"], (seq // TOK, TOK, kt, P), (0, 3, 2, 1)),
        "meta_t": lay(inputs["meta"], (n_meta, kt, P), (2, 1, 0)),
        "w_in": lay(lay(inputs["a_w_in"], (kt, P, GROUPS, CW), (2, 1, 0, 3))[::-1], (GROUPS, P, kt, CW), (0, 1, 2, 3)),
        "w_group_t": lay(inputs["a_w_group"], (GROUPS, CW, cp, P), (3, 0, 2, 1)).reshape(P, -1),
        "scale": lay(inputs["a_scale"], (kt, P), (1, 0)),
        "w_out": lay(inputs["a_w_out"], (GROUPS, cp, P, d), (0, 2, 1, 3)),
        "mix_g": np.ascontiguousarray(inputs["ln_mix_g"][0]),
        "mix_b": np.ascontiguousarray(inputs["ln_mix_b"][0]),
        "w_gu": lay(inputs["ffn_w_gu"], (kt, P, 2, ff // CW, CW), (3, 2, 1, 0, 4)),
        "w_down": lay(inputs["ffn_w_down"], (ff // P, P, d // TOK, TOK), (2, 1, 0, 3)),
        "ffn_g": np.ascontiguousarray(inputs["ln_ffn_g"][0]),
        "ffn_b": np.ascontiguousarray(inputs["ln_ffn_b"][0]),
    }
    nc = bacc.Bacc("TRN2", target_bir_lowering=False, num_devices=1)
    f32 = mb.dt.float32
    args = [nc.dram_tensor(n, a.shape, mb.dt.from_np(a.dtype), kind="ExternalInput").ap() for n, a in arrays.items()]
    args.append(nc.dram_tensor("out", (seq, d), f32, kind="ExternalOutput").ap())
    args.append(nc.dram_tensor("fold_dram", (GROUPS, P, kt // 2, TOK), f32, kind="Internal").ap())
    args.append(nc.dram_tensor("h_dram", (seq, d), f32, kind="Internal").ap())
    trunk(nc, *args)
    r = run_bass_kernel_spmd(nc, [arrays], core_ids=[0])
    return r.results[0]["out"].reshape(1, seq, d)
```
